# Optimizing a Trainium2 kernel written in Bass

```python
import math
import jax, jax.numpy as jnp
from jax import lax
import numpy as np

D_MODEL = 1024
BATCH = 1
SEQ = 256
DEPTH = 1

N_META = 16
CONV_W = D_MODEL // 2
CONV_GROUPS = 8
LRU_W = D_MODEL // 2
LRU_HEADS = 8
D_MIX = CONV_W + LRU_W
D_IN = 2 * CONV_W + 2 * LRU_W
CONV_K = 31
LRU_CONV_K = 4
RG_C = 8.0
N_EXPERTS = 32
TOP_K = 4
D_EXPERT = D_MODEL
SWIGLU_ALPHA = 1.702
SWIGLU_LIMIT = 7.0
NORM_EPS = 1e-6
LN_EPS = 1e-5

kernel_name = "hymba_conformer_rglru_moe_block"

def rms_norm(x, g):
    x32 = x.astype(jnp.float32)
    y = x32 * lax.rsqrt(jnp.mean(x32 * x32, axis=-1, keepdims=True) + NORM_EPS)
    return (y * g.astype(jnp.float32)).astype(x.dtype)

def layer_norm(x, g, b):
    x32 = x.astype(jnp.float32)
    mu = jnp.mean(x32, axis=-1, keepdims=True)
    xc = x32 - mu
    y = xc * lax.rsqrt(jnp.mean(xc * xc, axis=-1, keepdims=True) + LN_EPS)
    return (y * g.astype(jnp.float32) + b.astype(jnp.float32)).astype(x.dtype)

def causal_depthwise_conv(x, w, b):
    k = w.shape[0]
    xp = jnp.pad(x, ((0, 0), (k - 1, 0), (0, 0)))
    y = lax.conv_general_dilated(
        xp, w[:, None, :].astype(x.dtype), window_strides=(1,), padding="VALID",
        dimension_numbers=("NWC", "WIO", "NWC"), feature_group_count=x.shape[-1])
    return y + b.astype(x.dtype)

def conformer_conv_group(val, gate, dw_w, dw_b, ln_g, ln_b):
    u = val * jax.nn.sigmoid(gate)
    u = causal_depthwise_conv(u, dw_w, dw_b)
    u = layer_norm(u, ln_g, ln_b)
    return jax.nn.silu(u)

def _lru_combine(left, right):
    a1, b1 = left
    a2, b2 = right
    return a1 * a2, a2 * b1 + b2

def rg_lru(x, w_a, b_a, w_x, b_x, lam):
    bsz, t, c = x.shape
    xh = x.reshape(bsz, t, LRU_HEADS, c // LRU_HEADS)
    r = jax.nn.sigmoid(jnp.einsum("bthi,hij->bthj", xh, w_a).reshape(bsz, t, c) + b_a)
    i = jax.nn.sigmoid(jnp.einsum("bthi,hij->bthj", xh, w_x).reshape(bsz, t, c) + b_x)
    r32 = r.astype(jnp.float32)
    log_a = -RG_C * r32 * jax.nn.softplus(-lam.astype(jnp.float32))
    a = jnp.exp(log_a)
    mult = jnp.sqrt(-jnp.expm1(2.0 * log_a))
    is_start = (jnp.arange(t) == 0)[None, :, None]
    mult = jnp.where(is_start, 1.0, mult)
    bterm = mult * (i.astype(jnp.float32) * x.astype(jnp.float32))
    _, h = lax.associative_scan(_lru_combine, (a, bterm), axis=1)
    return h.astype(x.dtype)

def griffin_group(xin, gin, conv_w, conv_b, w_a, b_a, w_x, b_x, lam):
    y = jax.nn.gelu(gin, approximate=True)
    u = causal_depthwise_conv(xin, conv_w, conv_b)
    u = rg_lru(u, w_a, b_a, w_x, b_x, lam)
    return u * y

def moe_ffn(u, w_router, b_router, w_gu, b_gu, w_down, b_down):
    bsz, t, d = u.shape
    tok = u.reshape(bsz * t, d)
    logits = (tok @ w_router + b_router).astype(jnp.float32)
    vals, idx = lax.top_k(logits, TOP_K)
    wts = jax.nn.softmax(vals, axis=-1)
    gates = jnp.einsum("nk,nke->ne", wts, jax.nn.one_hot(idx, N_EXPERTS, dtype=jnp.float32))
    gates = gates.astype(tok.dtype)

    def expert_step(acc, xs):
        wgu, bgu, wd, bd, g = xs
        hgu = tok @ wgu + bgu
        x_glu = jnp.minimum(hgu[:, 0::2], SWIGLU_LIMIT)
        x_lin = jnp.clip(hgu[:, 1::2], -SWIGLU_LIMIT, SWIGLU_LIMIT)
        act = x_glu * jax.nn.sigmoid(SWIGLU_ALPHA * x_glu) * (x_lin + 1.0)
        out = act @ wd + bd
        return acc + g[:, None] * out, None

    acc, _ = lax.scan(expert_step, jnp.zeros_like(tok), (w_gu, b_gu, w_down, b_down, gates.T))
    return acc.reshape(bsz, t, d)

def setup_inputs(seed: int = 0) -> dict:
    key = jax.random.key(seed)
    ks = jax.random.split(key, 24)
    f32 = jnp.float32
    L = DEPTH
    nrm = lambda k, shape, fan_in: jax.random.normal(k, shape, f32) * (fan_in ** -0.5)
    small = lambda k, shape, s=0.02: jax.random.normal(k, shape, f32) * s
    blk = LRU_W // LRU_HEADS
    u = jax.random.uniform(ks[14], (L, LRU_W), f32, 0.9, 0.999)
    a0 = u ** (1.0 / RG_C)
    lam = jnp.log(a0) - jnp.log1p(-a0)
    return {
        "x": jax.random.normal(ks[0], (BATCH, SEQ, D_MODEL), f32),
        "meta_tokens": jax.random.normal(ks[1], (N_META, D_MODEL), f32),
        "g_mix": 1.0 + small(ks[2], (L, D_MODEL)),
        "w_in": nrm(ks[3], (L, D_MODEL, D_IN), D_MODEL),
        "conv_dw_w": nrm(ks[4], (L, CONV_K, CONV_W), CONV_K),
        "conv_dw_b": small(ks[5], (L, CONV_W)),
        "conv_ln_g": 1.0 + small(ks[6], (L, CONV_W)),
        "conv_ln_b": small(ks[7], (L, CONV_W)),
        "lru_conv_w": nrm(ks[8], (L, LRU_CONV_K, LRU_W), LRU_CONV_K),
        "lru_conv_b": small(ks[9], (L, LRU_W)),
        "lru_wa": nrm(ks[10], (L, LRU_HEADS, blk, blk), blk),
        "lru_ba": small(ks[11], (L, LRU_W)),
        "lru_wx": nrm(ks[12], (L, LRU_HEADS, blk, blk), blk),
        "lru_bx": small(ks[13], (L, LRU_W)),
        "lru_lambda": lam,
        "w_out": nrm(ks[15], (L, D_MIX, D_MODEL), D_MIX),
        "g_ffn": 1.0 + small(ks[16], (L, D_MODEL)),
        "w_router": nrm(ks[17], (L, D_MODEL, N_EXPERTS), D_MODEL),
        "b_router": small(ks[18], (L, N_EXPERTS), 0.01),
        "w_gate_up": nrm(ks[19], (L, N_EXPERTS, D_MODEL, 2 * D_EXPERT), D_MODEL),
        "b_gate_up": small(ks[20], (L, N_EXPERTS, 2 * D_EXPERT)),
        "w_down": nrm(ks[21], (L, N_EXPERTS, D_EXPERT, D_MODEL), D_EXPERT),
        "b_down": small(ks[22], (L, N_EXPERTS, D_MODEL)),
        "g_final": 1.0 + small(ks[23], (D_MODEL,)),
    }

def reference(x, meta_tokens, g_mix, w_in, conv_dw_w, conv_dw_b, conv_ln_g, conv_ln_b,
              lru_conv_w, lru_conv_b, lru_wa, lru_ba, lru_wx, lru_bx, lru_lambda, w_out,
              g_ffn, w_router, b_router, w_gate_up, b_gate_up, w_down, b_down, g_final):
    bsz = x.shape[0]
    meta = jnp.broadcast_to(meta_tokens[None].astype(x.dtype), (bsz, N_META, D_MODEL))
    h = jnp.concatenate([meta, x], axis=1)
    for l in range(DEPTH):
        u = rms_norm(h, g_mix[l])
        z = u @ w_in[l]
        c_val, c_gate, r_x, r_gate = jnp.split(
            z, [CONV_W, 2 * CONV_W, 2 * CONV_W + LRU_W], axis=-1)
        conv_out = conformer_conv_group(c_val, c_gate, conv_dw_w[l], conv_dw_b[l],
                                        conv_ln_g[l], conv_ln_b[l])
        lru_out = griffin_group(r_x, r_gate, lru_conv_w[l], lru_conv_b[l], lru_wa[l], lru_ba[l],
                                lru_wx[l], lru_bx[l], lru_lambda[l])
        mix = jnp.concatenate([conv_out, lru_out], axis=-1)
        h = h + mix @ w_out[l]
        u = rms_norm(h, g_ffn[l])
        h = h + moe_ffn(u, w_router[l], b_router[l], w_gate_up[l], b_gate_up[l],
                        w_down[l], b_down[l])
    h = rms_norm(h, g_final)
    return h[:, N_META:]


_drawn_inputs = setup_inputs


def setup_inputs(seed=0):
    import zlib

    import numpy as np

    out = dict(_drawn_inputs(seed))
    spreads = {}
    factors = {'lru_ba': 14.985, 'lru_bx': 10.75, 'b_gate_up': 5.563, 'b_down': 6.398, 'g_final': 8.45}
    for name, (base, spread) in spreads.items():
        noise = np.random.default_rng([zlib.crc32(name.encode()), seed]).standard_normal(out[name].shape)
        drawn = base * np.exp(spread * noise) if base else spread * noise
        out[name] = __import__('jax').numpy.asarray(drawn.astype(out[name].dtype))
    for name, factor in factors.items():
        out[name] = (out[name] * factor).astype(out[name].dtype)
    return out
```

```python
import concourse.bass as bass
from concourse import mybir
from concourse.alu_op_type import AluOpType as ALU
from contextlib import ExitStack
import numpy as np

f32 = mybir.dt.float32
bf16 = mybir.dt.bfloat16
i32 = mybir.dt.int32
ACT = mybir.ActivationFunctionType
AX = mybir.AxisListType

P = 128
D = 1024
KD = D // P
META = 16
SEQ = 256
T = META + SEQ
TT = SEQ // P
CW = 512
CC = CW // P
TAPS = 31
LTAPS = 4
NE = 32
TOPK = 4
F2 = 2 * D
SLOTS = 64
EXTRA = SEQ // SLOTS - 1
CAND = EXTRA * NE
XCOLS = 16
ITEMS = NE + XCOLS
NEG_EPS, LN_EPS = 1e-6, 1e-5

V_CW, V_CB, V_LG, V_LB, V_LW, V_LCB, V_BA, V_BX, V_LAM = 0, 31, 32, 33, 34, 38, 39, 40, 41
NV = 42
BC = 256
NG = 2 * KD

C_ID, C_ONE, C_TRI, C_SLOT = 0, P, 2 * P, 3 * P
C_TRI96 = 4 * P
C_RR = C_TRI96 + CAND
C_THRB = C_RR + CAND
C_IOTA = C_THRB + CAND
C_EID = C_IOTA + XCOLS
C_THRC = C_EID + 1
C_COLS = C_THRC + 1


def constants():
    c = np.zeros((P, C_COLS), np.float32)
    r = np.arange(P)[:, None]
    c[:, C_ID:C_ID + P] = r == np.arange(P)
    c[:, C_ONE:C_ONE + P] = 1.0
    c[:, C_TRI:C_TRI + P] = r < np.arange(P)
    c[:, C_SLOT:C_SLOT + P] = np.arange(P) % SLOTS
    q = np.arange(CAND)
    c[:CAND, C_TRI96:C_TRI96 + CAND] = q[:, None] < q
    c[:CAND, C_RR:C_RR + CAND] = (q[:, None] % NE) == (q % NE)
    c[:, C_THRB:C_THRB + CAND] = SLOTS * (q // NE + 1)
    c[:, C_IOTA:C_IOTA + XCOLS] = np.arange(XCOLS)
    c[:CAND, C_EID] = q % NE
    c[:CAND, C_THRC] = SLOTS * (q // NE + 1)
    return c


def build(nc, x, meta, g_mix, w_in, cdw, cdb, clg, clb, lcw, lcb, lwa, lba, lwx, lbx, lam,
          w_out, g_ffn, w_router, b_router, w_gu, b_gu, w_dn, b_dn, g_final, const, out):
    ctx = ExitStack()
    with ctx:
        def sb(name, cols, dt=f32):
            return ctx.enter_context(nc.sbuf_tensor(name, [P, cols], dt))

        def sem(name):
            return ctx.enter_context(nc.semaphore(name))

        gu_ring = ctx.enter_context(nc.sbuf_tensor("gu_ring", [P, 2, KD, F2], f32))
        dn_ring = ctx.enter_context(nc.sbuf_tensor("dn_ring", [P, KD, D], f32))
        xh = ctx.enter_context(nc.sbuf_tensor("xh", [P, TT, D], f32))
        reg2 = sb("reg2", KD * T)
        reg3 = sb("reg3", KD * SEQ)
        reg4 = sb("reg4", CC * 302 + T + CC * SEQ + SEQ)
        reg5 = sb("reg5", F2 // 2)
        cst = sb("cst", C_COLS)
        colv = sb("colv", CC * NV + NG)
        stage = sb("stage", BC)
        wr = ctx.enter_context(nc.sbuf_tensor("wr", [P, KD, NE], f32))
        tiny = sb("tiny", 80)

        ident = cst[:, C_ID:C_ID + P]
        ones = cst[:, C_ONE:C_ONE + P]
        tri = cst[:, C_TRI:C_TRI + P]
        slot_no = cst[:, C_SLOT:C_SLOT + P]

        uT = reg2[:, :].rearrange("p (k t) -> p k t", k=KD)
        unat = reg3[:, :].rearrange("p (t d) -> p t d", t=TT)
        mixT = reg3[:, :].rearrange("p (k t) -> p k t", k=KD)
        scr = gu_ring[:, 0, 0:4, :].rearrange("p a b -> p (a b)")
        o = 0
        rx = scr[:, o:o + CC * 275].rearrange("p (c t) -> p c t", c=CC)
        o += CC * 275
        lru = []
        for _ in range(5):
            lru.append(scr[:, o:o + CC * T].rearrange("p (c t) -> p c t", c=CC))
            o += CC * T
        lu, ltau, li, rg, lr = lru
        metah = gu_ring[0:META, 1, KD - 1, 0:D]
        vrow = gu_ring[0:NV, 1, KD - 2, 0:CW]
        grow = gu_ring[0:NG, 1, KD - 2, CW:CW + P]
        o = 0
        gpad = reg4[:, o:o + CC * 302].rearrange("p (c t) -> p c t", c=CC)
        o += CC * 302
        sig = reg4[:, o:o + T]
        o += T
        yc = reg4[:, o:o + CC * SEQ].rearrange("p (c t) -> p c t", c=CC)
        o += CC * SEQ
        acc2 = reg4[:, o:o + SEQ]
        lnsq = gpad[:, :, 0:SEQ]
        bdiag = reg3[:, KD * SEQ // 2:].rearrange("p (c n) -> p c n", c=2 * CC)

        xn = reg2[:, 0:TT * D].rearrange("p (t d) -> p t d", t=TT)
        hT = reg3[:, :].rearrange("p (t k n) -> p t k n", t=TT, k=KD)
        biasp = reg5[0:3 * NE, :].bitcast(bf16)
        o = 0
        xgT = reg3[:, 0:512].rearrange("p (k s) -> p k s", k=KD)
        actv = reg3[:, 512:1024]
        xglu = reg3[:, 1024:1536]
        sigm = reg3[:, 1536:2048]
        lin = reg4[:, 0:512]
        actT = reg4[:, 512:1024]
        yv = reg4[:, 1024:1536]
        gT = reg4[:, 1536:1792]
        onehot = reg4[:, 1792:1920].rearrange("p (t s) -> p t s", t=TT)
        wonehot = reg4[:, 1920:2176].rearrange("p (t s) -> p t s", t=TT)
        tabs = reg4[:, 2176:]
        o = 0

        def small(n):
            nonlocal o
            o += n
            return tabs[:, o - n:o]
        post = small(TT * ITEMS).rearrange("p (t e) -> p t e", t=TT)
        gatet = small(TT * ITEMS).rearrange("p (t e) -> p t e", t=TT)
        selt = small(ITEMS)
        selb = small(SLOTS // 2).bitcast(bf16)
        qi = small(XCOLS + 1).bitcast(i32)
        rt = reg4[:, 0:1024]
        o = 0

        def rsmall(n):
            nonlocal o
            o += n
            return rt[:, o - n:o]

        def two(a, n):
            return a.rearrange("p (t e) -> p t e", t=TT)
        lg = two(rsmall(TT * NE), NE)
        mx = two(rsmall(TT * 8), 8)
        gt = two(rsmall(TT * NE), NE)
        eq = two(rsmall(TT * NE), NE)
        ceq = two(rsmall(TT * NE), NE)
        ex = two(rsmall(TT * NE), NE)
        cnt = two(rsmall(TT), 1)
        den = two(rsmall(TT), 1)
        mask = two(rsmall(TT * NE), NE)
        brow = tiny[:, 48:48 + NE]
        zeros = reg3[:, 1536:2048].bitcast(bf16)
        mask3 = rsmall(TT * CAND).rearrange("p (t b e) -> p t b e", t=TT, b=EXTRA)
        fx = rsmall(2)
        sel96 = rsmall(XCOLS)
        candT = [reg3[0:CAND, 0:SEQ], reg3[0:CAND, SEQ:2 * SEQ]]
        cand = [reg3[:, 512:512 + TT * CAND].rearrange("p (t q) -> p t q", t=TT),
                reg3[:, 1024:1024 + TT * CAND].rearrange("p (t q) -> p t q", t=TT)]
        ssq = tiny[:, 0:3]
        rstd = tiny[:, 3:6]
        sp4 = tiny[:, 8:12]
        spt = [tiny[:, 12 + 4 * i:16 + 4 * i] for i in range(4)]
        ssq2, rstd2 = tiny[:, 28:30], tiny[:, 30:32]
        ssq3, rstd3 = tiny[:, 32:34], tiny[:, 34:36]
        gfin = gu_ring[:, 1, 0, 0:D]
        bdn = gu_ring[0:NE, 1, 1, 0:D]
        outb = gu_ring[:, 1, 2, :].rearrange("p (t d) -> p t d", t=TT)
        gtT = gu_ring[0:NE, 1, 3, 0:SEQ]

        bank = [ctx.enter_context(nc.psum_tensor(f"bank{i}", [P, 512], f32)) for i in range(8)]
        accb = [[bank[0], bank[1]], [bank[2], bank[3]]]
        gub = [bank[4], bank[5]]
        tb, db = bank[6], bank[7]

        def col(v, c):
            return colv[:, c * NV + v:c * NV + v + 1]

        def gcol(k):
            return colv[:, CC * NV + k:CC * NV + k + 1]

        x_in, meta_in, vec_in, cst_in = sem("x_in"), sem("meta_in"), sem("vec_in"), sem("cst_in")
        lruw_in, route_in = sem("lruw_in"), sem("route_in")
        win_in = [sem(f"win_in{p}") for p in range(KD)]
        wout_in = [sem(f"wout_in{j}") for j in range(4)]
        gu_in = [[sem(f"gu_in{s}_{j}") for j in range(KD)] for s in range(2)]
        dn_in = [sem(f"dn_in{j}") for j in range(4)]
        gu_used = [sem("gu_used0"), sem("gu_used1")]
        dn_used = sem("dn_used")
        wout_used = sem("wout_used")
        dv = sem("dve_step")
        pool_step, bias_in, bd_zero = sem("pool_step"), sem("bias_in"), sem("bd_zero")
        vecT, vec_ok = sem("vecT"), sem("vec_ok")
        ss_act, ms_ok, rt_ok, un_ok = sem("ss_act"), sem("ms_ok"), sem("rt_ok"), sem("un_ok")
        uT_ps, uT_dve, uT_act = sem("uT_ps"), sem("uT_dve"), sem("uT_act")
        z_ps, z_dve, z_act = sem("z_ps"), sem("z_dve"), sem("z_act")
        sp_act, sp_dve = sem("sp_act"), sem("sp_dve")
        lu_ok, lg_ps, lg_act = sem("lu_ok"), sem("lg_ps"), sem("lg_act")
        gelu_ok, sq_ok, rinv_ok = sem("gelu_ok"), sem("sq_ok"), sem("rinv_ok")
        yc_ok, mean_ps, xc_ok, sq2_ok, var_ps = (sem(n) for n in ("yc_ok", "mean_ps", "xc_ok", "sq2_ok", "var_ps"))
        lnv_ok, lns_ok, yn_ok, lsig_ok = sem("lnv_ok"), sem("lns_ok"), sem("yn_ok"), sem("lsig_ok")
        mix_ok, h_ps, h_ok = sem("mix_ok"), sem("h_ps"), sem("h_ok")
        ss2_ok, ms2_ok, rt2_ok = sem("ss2_ok"), sem("ms2_ok"), sem("rt2_ok")
        hT_ps, hT_ok, wr_ok, lg2_ps = sem("hT_ps"), sem("hT_ok"), sem("wr_ok"), sem("lg2_ps")
        ex_in, ex_ok, mask_ok, pos_ps = sem("ex_in"), sem("ex_ok"), sem("mask_ok"), sem("pos_ps")
        x_dve, x_pe, q_ok = sem("x_dve"), sem("x_pe"), sem("q_ok")
        oh_ok, gath_ps, xg_ok = sem("oh_ok"), sem("gath_ps"), sem("xg_ok")
        glu_ok, gu_read, sg_ok, act_ok = sem("glu_ok"), sem("gu_read"), sem("sg_ok"), sem("act_ok")
        gT_ps, gT_ok, aT_ps, aT_ok = sem("gT_ps"), sem("gT_ok"), sem("aT_ps"), sem("aT_ok")
        y_ps, y_ok, acc_ps = sem("y_ps"), sem("y_ok"), sem("acc_ps")
        tail_in, fin_dve, gtT_ps, bd_ps, ms3_ok, rt3_ok, out_ok, out_done = (
            sem(n) for n in ("tail_in", "fin_dve", "gtT_ps", "bd_ps", "ms3_ok", "rt3_ok", "out_ok", "out_done"))

        w_in_v = w_in[0].rearrange("(k p) (b c n) -> p k b c n", p=P, b=4, c=CC)
        w_out_v = w_out[0].rearrange("(k p) n -> p k n", p=P)
        gu_v = w_gu[0].rearrange("e (k p) n -> p e k n", p=P)
        dn_v = w_dn[0].rearrange("e (k p) n -> p e k n", p=P)

        block = ctx.enter_context(nc.Block())

        @block.sync
        def _(sp):
            sp.dma_start(xh[:, 0, :], x[0, 0:P, :]).then_inc(x_in, 16)
            sp.dma_start(xh[:, 1, :], x[0, P:2 * P, :]).then_inc(x_in, 16)
            for p in range(KD):
                piece = gu_ring[:, 0, p, :].rearrange("p (k b n) -> p k b n", k=KD, b=2)
                for b in range(2):
                    sp.dma_start(piece[:, :, b, :], w_in_v[:, :, 2 * (p // CC) + b, p % CC, :]).then_inc(win_in[p], 16)
            for j in range(4):
                sp.dma_start(dn_ring[:, 2 * j:2 * j + 2, :], w_out_v[:, 2 * j:2 * j + 2, :]).then_inc(wout_in[j], 16)

            def gu_load(s, e, done):
                for j in range(KD):
                    sp.wait_ge(gu_used[s], done * KD + (j + 1))
                    sp.dma_start(gu_ring[:, s, j, :], gu_v[:, e, j, :]).then_inc(gu_in[s][j], 16)

            def dn_load(e, done):
                for j in range(4):
                    if j < 3:
                        sp.wait_ge(dn_used, done * 3 + (j + 1))
                    else:
                        sp.wait_ge(y_ps, done + 1)
                    sp.dma_start(dn_ring[:, 2 * j:2 * j + 2, :], dn_v[:, e, 2 * j:2 * j + 2, :]).then_inc(dn_in[j], 16)

            sp.wait_ge(vecT, 1)
            sp.wait_ge(uT_ps, KD)
            for j in range(KD):
                sp.dma_start(gu_ring[:, 1, j, :], gu_v[:, 0, j, :]).then_inc(gu_in[1][j], 16)
            for j in range(4):
                if j < 3:
                    sp.wait_ge(wout_used, j + 1)
                else:
                    sp.wait_ge(h_ps, 2 * TT)
                sp.dma_start(dn_ring[:, 2 * j:2 * j + 2, :], dn_v[:, 0, 2 * j:2 * j + 2, :]).then_inc(dn_in[j], 16)
            for j in range(KD):
                sp.wait_ge(z_ps, j + 1)
                sp.dma_start(gu_ring[:, 0, j, :], gu_v[:, 1, j, :]).then_inc(gu_in[0][j], 16)
            dn_load(1, 0)
            with sp.Fori(1, NE // 2) as g:
                gu_load(1, g * 2, g - 1)
                dn_load(g * 2, g * 2 - 1)
                gu_load(0, g * 2 + 1, g - 1)
                dn_load(g * 2 + 1, g * 2)
            sp.wait_ge(gu_used[1], NE // 2 * KD)
            sp.dma_start(gfin, g_final.partition_broadcast(P)).then_inc(tail_in, 16)
            sp.dma_start(bdn, b_dn[0]).then_inc(tail_in, 16)
            sp.wait_ge(q_ok, 1)
            n_x = sp.value_load(qi[0:1, XCOLS:XCOLS + 1], min_val=0, max_val=XCOLS - 1)
            with sp.If(n_x > 0):
                with sp.Fori(0, n_x) as q:
                    e = sp.value_load(qi[0:1, bass.ds(q, 1)], min_val=0, max_val=NE - 1)
                    gu_load(0, e, q + (NE // 2 - 1))
                    dn_load(e, q + (NE - 1))
            for t in range(TT):
                sp.wait_ge(out_ok, t + 1)
                sp.dma_start(out[0, t * P:(t + 1) * P, :], outb[:, t, :]).then_inc(out_done, 16)
            sp.wait_ge(out_done, 16 * TT)

        @block.gpsimd
        def _(pool):
            pool.dma_start(metah, meta).then_inc(meta_in, 16)
            pool.dma_start(cst[:, :], const).then_inc(cst_in, 16)
            rows = [(V_CW, TAPS, cdw[0]), (V_CB, 1, cdb), (V_LG, 1, clg), (V_LB, 1, clb), (V_LW, LTAPS, lcw[0]),
                    (V_LCB, 1, lcb), (V_BA, 1, lba), (V_BX, 1, lbx), (V_LAM, 1, lam)]
            for r, n, src in rows:
                pool.dma_start(vrow[r:r + n, :], src).then_inc(vec_in, 16)
            pool.dma_start(grow[0:KD, :], g_mix[0].rearrange("(k n) -> k n", k=KD)).then_inc(vec_in, 16)
            pool.dma_start(grow[KD:2 * KD, :], g_ffn[0].rearrange("(k n) -> k n", k=KD)).then_inc(vec_in, 16)
            pool.dma_start(wr[:, :, :], w_router[0].rearrange("(k p) e -> p k e", p=P)).then_inc(route_in, 16)
            pool.dma_start(brow, b_router[0].partition_broadcast(P)).then_inc(route_in, 16)
            pool.wait_ge(uT_ps, KD)
            nc.gpsimd.memset(bdiag[:, :, :], 0.0).then_inc(bd_zero, 1)
            pool.wait_ge(bd_zero, 1)
            for w, src in enumerate((lwa, lwx)):
                s4 = src[0].rearrange("(c h) i j -> h i c j", h=2)
                for h in range(2):
                    pool.dma_start(bdiag[64 * h:64 * h + 64, CC * w:CC * (w + 1), 64 * h:64 * h + 64], s4[h]).then_inc(lruw_in, 16)
            steps = 0
            for c in range(F2 // BC):
                at = slice(BC * c, BC * c + BC)
                for part in range(3):
                    pool.dma_start(stage[part * NE:(part + 1) * NE, :], b_gu[0, :, at]).then_inc(bias_in, 16)
                pool.wait_ge(bias_in, 48 * (c + 1))
                for part in range(3):
                    rows_ = slice(part * NE, (part + 1) * NE)
                    for i in range(part + 1):
                        nc.gpsimd.tensor_copy(biasp[rows_, at], stage[rows_, :]).then_inc(pool_step, 1)
                        steps += 1
                        pool.wait_ge(pool_step, steps)
                        if i < part:
                            nc.gpsimd.tensor_tensor(stage[rows_, :], stage[rows_, :], biasp[rows_, at], ALU.subtract).then_inc(pool_step, 1)
                            steps += 1
                            pool.wait_ge(pool_step, steps)

        bias_steps = F2 // BC * 9

        @block.scalar
        def _(act):
            act.wait_ge(x_in, 32)
            nc.scalar.activation(unat[:, 1, :], xh[:, 1, :], ACT.Square, accum_out=ssq[:, 1:2]).then_inc(ss_act, 1)
            act.wait_ge(ms_ok, 1)
            nc.scalar.activation(rstd, rstd, ACT.Sqrt).then_inc(rt_ok, 1)
            act.wait_ge(sp_dve, 1)
            nc.scalar.activation(spt[1], spt[0], ACT.Exp, scale=-1.0).then_inc(sp_act, 1)
            act.wait_ge(vec_ok, 1)
            for k in range(1, KD, 2):
                act.wait_ge(uT_ps, k + 1)
                nc.scalar.activation(uT[:, k, :], bank[k][:, 0:T], ACT.Copy, scale=gcol(k)).then_inc(uT_act, 1)
            for c in range(CC):
                act.wait_ge(z_ps, c + 1)
                if c:
                    act.wait_ge(z_dve, c)
                nc.scalar.activation(sig, bank[2 * (c % 2) + 1][:, 0:T], ACT.Sigmoid).then_inc(z_act, 1)
            for c in range(CC):
                act.wait_ge(z_ps, CC + c + 1)
                b = 2 * (c % 2)
                nc.scalar.activation(rx[:, c, 3:3 + T], bank[b][:, 0:T], ACT.Copy).then_inc(z_act, 1)
                nc.scalar.activation(rg[:, c, :], bank[b + 1][:, 0:T], ACT.Copy).then_inc(z_act, 1)
            act.wait_ge(sp_dve, 2)
            for c in range(CC):
                act.wait_ge(lg_ps, c + 1)
                nc.scalar.activation(ltau[:, c, :], bank[6][:, 0:T], ACT.Sigmoid, bias=col(V_BA, c)).then_inc(lg_act, 1)
                nc.scalar.activation(li[:, c, :], bank[7][:, 0:T], ACT.Sigmoid, bias=col(V_BX, c)).then_inc(lg_act, 1)
                act.wait_ge(lg_act, 3 * c + 1)
                nc.scalar.activation(ltau[:, c, :], ltau[:, c, :], ACT.Tanh, scale=sp4[:, c:c + 1]).then_inc(lg_act, 1)
            act.wait_ge(rinv_ok, 1)
            act.wait_ge(lg_act, 3 * CC)
            nc.scalar.activation(ltau[:, :, :], ltau[:, :, :], ACT.Sqrt, scale=4.0).then_inc(sq_ok, 1)
            act.wait_ge(xc_ok, 1)
            nc.scalar.activation(lnsq, yc[:, :, :], ACT.Square).then_inc(sq2_ok, 1)
            act.wait_ge(lnv_ok, 1)
            nc.scalar.activation(acc2, acc2, ACT.Sqrt).then_inc(lns_ok, 1)
            act.wait_ge(z_act, CC + 2 * CC)
            nc.scalar.activation(rg[:, :, :], rg[:, :, :], ACT.Gelu_apprx_tanh).then_inc(gelu_ok, 1)
            act.wait_ge(yn_ok, 1)
            for c in range(CC):
                nc.scalar.activation(lnsq[:, c, :], yc[:, c, :], ACT.Sigmoid, bias=col(V_LB, c), scale=col(V_LG, c)).then_inc(lsig_ok, 1)
            for t in range(TT):
                act.wait_ge(h_ok, 2 * t + 2)
                nc.scalar.activation(xn[:, t, :], xh[:, t, :], ACT.Square, accum_out=ssq2[:, t:t + 1]).then_inc(ss2_ok, 1)
            act.wait_ge(ms2_ok, 1)
            nc.scalar.activation(rstd2, rstd2, ACT.Sqrt).then_inc(rt2_ok, 1)
            for t in range(TT):
                act.wait_ge(hT_ps, 2 * t + 2)
                for b in range(2):
                    nc.scalar.activation(hT[:, t, 4 * b:4 * b + 4, :], bank[4 + 2 * t + b][:, :].rearrange("p (k n) -> p k n", k=4), ACT.Copy).then_inc(hT_ok, 1)
            act.wait_ge(ex_in, 1)
            nc.scalar.activation(ex[:, :, :], ex[:, :, :], ACT.Exp).then_inc(ex_ok, 1)

            def expert(n):
                act.wait_ge(gT_ps, n + 1)
                act.wait_ge(acc_ps, n + 1)
                nc.scalar.activation(gT, tb[:, 0:SEQ], ACT.Copy).then_inc(gT_ok, 1)
                act.wait_ge(glu_ok, n + 1)
                nc.scalar.activation(sigm, xglu, ACT.Sigmoid, scale=1.702).then_inc(sg_ok, 1)
                act.wait_ge(aT_ps, n + 1)
                nc.scalar.activation(actT, tb[:, :], ACT.Copy).then_inc(aT_ok, 1)
                act.wait_ge(y_ps, n + 1)
                nc.scalar.activation(yv, db[:, :], ACT.Copy).then_inc(y_ok, 1)

            with act.Fori(0, NE) as n:
                expert(n)
            act.wait_ge(q_ok, 1)
            n_x = act.value_load(qi[0:1, XCOLS:XCOLS + 1], min_val=0, max_val=XCOLS - 1)
            with act.If(n_x > 0):
                with act.Fori(0, n_x) as q:
                    expert(q + NE)
            act.wait_ge(ms3_ok, 1)
            nc.scalar.activation(rstd3, rstd3, ACT.Sqrt).then_inc(rt3_ok, 1)

        @block.vector
        def _(v):
            step = [0]

            def link(ins):
                step[0] += 1
                ins.then_inc(dv, 1)
                v.wait_ge(dv, step[0])

            def mark(ins):
                step[0] += 1
                ins.then_inc(dv, 1)
                return step[0]

            V = nc.vector
            link(V.memset(ssq[:, 2:3], 1.0))
            link(V.memset(gpad[:, :, 0:TAPS - 1], 0.0))
            v.wait_ge(meta_in, 16)
            link(V.tensor_tensor_reduce(out=reg2[0:META, 0:D], in0=metah, in1=metah, scale=1.0, scalar=0.0,
                                        op0=ALU.mult, op1=ALU.add, accum_out=ssq[0:META, 2:3]))
            v.wait_ge(x_in, 32)
            link(V.tensor_tensor_reduce(out=unat[:, 0, :], in0=xh[:, 0, :], in1=xh[:, 0, :], scale=1.0, scalar=0.0,
                                        op0=ALU.mult, op1=ALU.add, accum_out=ssq[:, 0:1]))
            v.wait_ge(ss_act, 1)
            V.tensor_scalar(rstd, ssq, 1.0 / D, NEG_EPS, ALU.mult, ALU.add).then_inc(ms_ok, 1)
            v.wait_ge(rt_ok, 1)
            link(V.reciprocal(rstd, rstd))
            V.tensor_scalar(metah, metah, rstd[0:META, 2:3], None, ALU.mult).then_inc(un_ok, 1)
            for t in range(TT):
                V.tensor_scalar(unat[:, t, :], xh[:, t, :], rstd[:, t:t + 1], None, ALU.mult).then_inc(un_ok, 1)
            v.wait_ge(vecT, 1)
            V.tensor_copy(colv[:, :], bank[7][:, 0:CC * NV + NG]).then_inc(vec_ok, 1)
            v.wait_ge(vec_ok, 1)
            lamc = colv[:, 0:CC * NV].rearrange("p (c n) -> p c n", c=CC)[:, :, V_LAM]
            link(V.tensor_scalar(spt[3], lamc, -1.0, 0.0, ALU.mult, ALU.max))
            link(V.tensor_scalar(spt[2], lamc, 0.0, None, ALU.max))
            V.tensor_tensor(spt[0], spt[3], spt[2], ALU.add).then_inc(sp_dve, 1)
            for k in range(0, KD, 2):
                v.wait_ge(uT_ps, k + 1)
                V.tensor_scalar(uT[:, k, :], bank[k][:, 0:T], gcol(k), None, ALU.mult).then_inc(uT_dve, 1)
            v.wait_ge(sp_act, 1)
            link(V.tensor_scalar(spt[2], spt[1], 2.0, None, ALU.add))
            link(V.reciprocal(spt[2], spt[2]))
            link(V.tensor_tensor(spt[1], spt[1], spt[2], ALU.mult))
            link(V.tensor_tensor(spt[2], spt[1], spt[1], ALU.mult))
            link(V.memset(spt[0], 1.0 / 17))
            for d in (15, 13, 11, 9, 7, 5, 3, 1):
                link(V.tensor_tensor(spt[0], spt[0], spt[2], ALU.mult))
                link(V.tensor_scalar(spt[0], spt[0], 1.0 / d, None, ALU.add))
            link(V.tensor_tensor(spt[0], spt[0], spt[1], ALU.mult))
            link(V.scalar_tensor_tensor(spt[0], spt[0], 2.0, spt[3], ALU.mult, ALU.add))
            V.tensor_scalar(sp4, spt[0], 4.0, None, ALU.mult).then_inc(sp_dve, 1)

            def glu(c):
                v.wait_ge(z_act, c + 1)
                V.tensor_tensor(gpad[:, c, TAPS - 1:TAPS - 1 + T], bank[2 * (c % 2)][:, 0:T], sig, ALU.mult).then_inc(z_dve, 1)

            glu(0)
            for c in range(CC):
                v.wait_ge(z_dve, c + 1)
                two_sums = [yc[:, c, :], acc2]
                last = [0, 0]
                for k in range(TAPS):
                    src = gpad[:, c, META + k:META + k + SEQ]
                    a = two_sums[k % 2]
                    if k == 0:
                        last[0] = mark(V.tensor_scalar(a, src, col(V_CW, c), col(V_CB, c), ALU.mult, ALU.add))
                    elif k == 1:
                        last[1] = mark(V.tensor_scalar(a, src, col(V_CW + 1, c), None, ALU.mult))
                    else:
                        v.wait_ge(dv, last[k % 2])
                        last[k % 2] = mark(V.scalar_tensor_tensor(a, src, col(V_CW + k, c), a, ALU.mult, ALU.add))
                    if k == 20 and c + 1 < CC:
                        glu(c + 1)
                v.wait_ge(dv, step[0])
                V.tensor_tensor(yc[:, c, :], yc[:, c, :], acc2, ALU.add).then_inc(yc_ok, 1)
                v.wait_ge(yc_ok, c + 1)
            v.wait_ge(z_ps, CC)
            link(V.memset(rx[:, :, 0:3], 0.0))
            for c in range(CC):
                v.wait_ge(z_act, CC + 2 * c + 2)
                link(V.tensor_scalar(lu[:, c, :], rx[:, c, 0:T], col(V_LW, c), col(V_LCB, c), ALU.mult, ALU.add))
                for k in range(1, LTAPS):
                    ins = V.scalar_tensor_tensor(lu[:, c, :], rx[:, c, k:k + T], col(V_LW + k, c), lu[:, c, :], ALU.mult, ALU.add)
                    if k < LTAPS - 1:
                        link(ins)
                    else:
                        ins.then_inc(lu_ok, 1)
            v.wait_ge(mean_ps, 1)
            mean = bank[4][:, 0:SEQ].unsqueeze(1).to_broadcast([P, CC, SEQ])
            V.scalar_tensor_tensor(yc[:, :, :], mean, -1.0 / CW, yc[:, :, :], ALU.mult, ALU.add).then_inc(xc_ok, 1)
            v.wait_ge(lg_act, 3 * CC)
            link(V.tensor_scalar(lr[:, :, :], ltau[:, :, :], 1.0, None, ALU.add))
            V.reciprocal(lr[:, :, :], lr[:, :, :]).then_inc(rinv_ok, 1)
            v.wait_ge(lu_ok, CC)
            link(V.tensor_tensor(li[:, :, :], li[:, :, :], lu[:, :, :], ALU.mult))
            v.wait_ge(var_ps, 1)
            V.tensor_scalar(acc2, bank[5][:, 0:SEQ], 1.0 / CW, LN_EPS, ALU.mult, ALU.add).then_inc(lnv_ok, 1)
            v.wait_ge(sq_ok, 1)
            v.wait_ge(rinv_ok, 1)
            link(V.tensor_tensor(ltau[:, :, :], ltau[:, :, :], lr[:, :, :], ALU.mult))
            link(V.memset(ltau[:, :, 0:1], 1.0))
            link(V.tensor_tensor(li[:, :, :], li[:, :, :], ltau[:, :, :], ALU.mult))
            link(V.tensor_scalar(lr[:, :, :], lr[:, :, :], 2.0, -1.0, ALU.mult, ALU.add))
            v.wait_ge(lns_ok, 1)
            link(V.reciprocal(acc2, acc2))
            V.tensor_tensor(yc[:, :, :], yc[:, :, :], acc2.unsqueeze(1).to_broadcast([P, CC, SEQ]), ALU.mult).then_inc(yn_ok, 1)
            for c in range(CC):
                link(V.tensor_tensor_scan(lu[:, c, :], lr[:, c, :], li[:, c, :], 0.0, ALU.mult, ALU.add))
            v.wait_ge(lsig_ok, CC)
            for c in range(CC):
                link(V.tensor_scalar(yc[:, c, :], yc[:, c, :], col(V_LG, c), col(V_LB, c), ALU.mult, ALU.add))
            V.tensor_tensor(mixT[:, 0:CC, :], yc[:, :, :], lnsq, ALU.mult).then_inc(mix_ok, 1)
            v.wait_ge(gelu_ok, 1)
            V.tensor_tensor(mixT[:, CC:, :], lu[:, :, META:], rg[:, :, META:], ALU.mult).then_inc(mix_ok, 1)
            v.wait_ge(route_in, 32)
            for k in range(KD):
                ins = V.tensor_scalar(wr[:, k, :], wr[:, k, :], gcol(KD + k), None, ALU.mult)
                if k < KD - 1:
                    link(ins)
            ins.then_inc(wr_ok, 1)
            for t in range(TT):
                for b in range(2):
                    v.wait_ge(h_ps, 2 * t + b + 1)
                    V.tensor_tensor(xh[:, t, 512 * b:512 * b + 512], bank[2 * t + b][:, :], xh[:, t, 512 * b:512 * b + 512], ALU.add).then_inc(h_ok, 1)
            v.wait_ge(ss2_ok, TT)
            V.tensor_scalar(rstd2, ssq2, 1.0 / D, NEG_EPS, ALU.mult, ALU.add).then_inc(ms2_ok, 1)
            v.wait_ge(rt2_ok, 1)
            link(V.reciprocal(rstd2, rstd2))
            v.wait_ge(lg2_ps, 1)
            for t in range(TT):
                link(V.scalar_tensor_tensor(lg[:, t, :], bank[0][:, NE * t:NE * (t + 1)], rstd2[:, t:t + 1], brow, ALU.mult, ALU.add))
            for t in range(TT):
                link(V.max(mx[:, t, :], lg[:, t, :]))
            V.tensor_tensor(ex[:, :, :], lg[:, :, :], mx[:, :, 0:1].to_broadcast([P, TT, NE]), ALU.subtract).then_inc(ex_in, 1)
            v4 = mx[:, :, TOPK - 1:TOPK].to_broadcast([P, TT, NE])
            link(V.tensor_tensor(gt[:, :, :], lg[:, :, :], v4, ALU.is_gt))
            link(V.tensor_tensor(eq[:, :, :], lg[:, :, :], v4, ALU.is_equal))
            link(V.tensor_reduce(cnt[:, :, 0], gt[:, :, :], axis=AX.X, op=ALU.add))
            for t in range(TT):
                link(V.tensor_tensor_scan(ceq[:, t, :], ones[:, 0:NE], eq[:, t, :], 0.0, ALU.mult, ALU.add))
            link(V.tensor_tensor(ceq[:, :, :], ceq[:, :, :], cnt[:, :, 0:1].to_broadcast([P, TT, NE]), ALU.add))
            link(V.scalar_tensor_tensor(eq[:, :, :], ceq[:, :, :], float(TOPK), eq[:, :, :], ALU.is_le, ALU.mult))
            V.tensor_tensor(mask[:, :, :], gt[:, :, :], eq[:, :, :], ALU.add).then_inc(mask_ok, 1)
            v.wait_ge(ex_ok, 1)
            v.wait_ge(mask_ok, 1)
            link(V.tensor_tensor(ex[:, :, :], ex[:, :, :], mask[:, :, :], ALU.mult))
            link(V.tensor_reduce(den[:, :, 0], ex[:, :, :], axis=AX.X, op=ALU.add))
            link(V.reciprocal(den[:, :, :], den[:, :, :]))
            link(V.tensor_tensor(gatet[:, :, 0:NE], ex[:, :, :], den[:, :, 0:1].to_broadcast([P, TT, NE]), ALU.mult))
            for t in range(TT):
                link(V.tensor_scalar(xn[:, t, :], xh[:, t, :], rstd2[:, t:t + 1], None, ALU.mult))
            v.wait_ge(pos_ps, 1)
            pos_v = bank[1][:, 0:TT * NE].rearrange("p (t e) -> p t e", t=TT)
            link(V.scalar_tensor_tensor(post[:, :, 0:NE], pos_v, 1.0, mask[:, :, :], ALU.add, ALU.mult))
            link(V.tensor_scalar(post[:, :, 0:NE], post[:, :, 0:NE], -1.0, None, ALU.add))
            for b in range(3):
                link(V.tensor_copy(selt[b * NE:(b + 1) * NE, 0:NE], ident[b * NE:(b + 1) * NE, b * NE:(b + 1) * NE]))

            for b in range(EXTRA):
                for t in range(TT):
                    link(V.tensor_copy(mask3[:, t, b, :], mask[:, t, :]))
                    link(V.tensor_scalar(cand[0][:, t, b * NE:(b + 1) * NE], post[:, t, 0:NE], -float(SLOTS * (b + 1)), None, ALU.add))
                    link(V.tensor_copy(cand[1][:, t, b * NE:(b + 1) * NE], gatet[:, t, 0:NE]))
            V.tensor_copy(fx[0:1, 0:1], ident[0:1, 0:1]).then_inc(x_dve, 1)
            v.wait_ge(x_pe, 1)
            c9 = slice(0, CAND)
            V.tensor_scalar(fx[c9, 0:1], bank[2][c9, 0:1], cst[c9, C_THRC:C_THRC + 1], None, ALU.is_gt).then_inc(x_dve, 1)
            v.wait_ge(x_pe, 2)
            link(V.tensor_copy(fx[c9, 1:2], bank[2][c9, 1:2]))
            V.tensor_scalar(sel96[c9, :], cst[c9, C_IOTA:C_IOTA + XCOLS], fx[c9, 1:2], fx[c9, 0:1], ALU.is_equal, ALU.mult).then_inc(x_dve, 1)
            v.wait_ge(x_pe, 3)
            for i in range(2):
                V.tensor_copy(candT[i], bank[3][c9, i * SEQ:(i + 1) * SEQ]).then_inc(x_dve, 1)
            v.wait_ge(x_pe, 4)
            for i, table in enumerate((post, gatet)):
                src = bank[2][:, 64 + 32 * i:64 + 32 * i + TT * XCOLS].rearrange("p (t q) -> p t q", t=TT)
                link(V.tensor_copy(table[:, :, NE:], src))
            link(V.tensor_copy(selt[c9, NE:], bank[2][c9, 128:128 + XCOLS]))
            V.memset(zeros, 0.0).then_inc(gu_read, 1)
            v.wait_ge(gu_read, 1)
            V.tensor_copy(qi[0:1, :], bank[2][0:1, 160:160 + XCOLS + 1]).then_inc(q_ok, 1)

            def one_hot(n):
                for t in range(TT):
                    ins = V.tensor_scalar(onehot[:, t, :], slot_no[:, 0:SLOTS], post[:, t, bass.ds(n, 1)], None, ALU.is_equal)
                ins.then_inc(oh_ok, 1)

            def gathered(n):
                v.wait_ge(gath_ps, n + 1)
                V.tensor_tensor(xgT[:, :, :], db[:, :].rearrange("p (k s) -> p k s", k=KD),
                                colv[:, CC * NV + KD:].unsqueeze(2).to_broadcast([P, KD, SLOTS]), ALU.mult).then_inc(xg_ok, 1)
                V.tensor_scalar(selb[0:CAND, :], ones[0:CAND, 0:SLOTS], selt[0:CAND, bass.ds(n, 1)], None, ALU.mult).then_inc(xg_ok, 1)

            one_hot(0)
            gathered(0)
            base = step[0]

            def expert(n, s, use):
                one_hot(n + 1)
                for t in range(TT):
                    ins = V.tensor_scalar(wonehot[:, t, :], slot_no, post[:, t, bass.ds(n, 1)], gatet[:, t, bass.ds(n, 1)], ALU.is_equal, ALU.mult)
                ins.then_inc(oh_ok, 1)
                v.wait_ge(gu_used[s], use * KD)
                for b in range(2):
                    glu_v = gub[b][:, :].rearrange("p (n two) -> p n two", two=2)
                    h = slice(256 * b, 256 * b + 256)
                    ins = V.tensor_scalar(xglu[:, h], glu_v[:, :, 0], 7.0, None, ALU.min)
                ins.then_inc(glu_ok, 1)
                for b in range(2):
                    glu_v = gub[b][:, :].rearrange("p (n two) -> p n two", two=2)
                    h = slice(256 * b, 256 * b + 256)
                    ins = V.tensor_scalar(lin[:, h], glu_v[:, :, 1], 7.0, -7.0, ALU.min, ALU.max)
                ins.then_inc(gu_read, 1)
                v.wait_ge(gu_read, n + 2)
                v.wait_ge(glu_ok, n + 1)
                V.scalar_tensor_tensor(lin, lin, 1.0, xglu, ALU.add, ALU.mult).then_inc(dv, 1)
                v.wait_ge(dv, n + (base + 1))
                v.wait_ge(sg_ok, n + 1)
                V.tensor_tensor(actv, lin, sigm, ALU.mult).then_inc(act_ok, 1)
                gathered(n + 1)

            with v.Fori(0, NE // 2) as g:
                expert(g * 2, 1, g + 1)
                expert(g * 2 + 1, 0, g + 1)
            v.wait_ge(q_ok, 1)
            n_x = v.value_load(qi[0:1, XCOLS:XCOLS + 1], min_val=0, max_val=XCOLS - 1)
            with v.If(n_x > 0):
                with v.Fori(0, n_x) as q:
                    expert(q + NE, 0, q + (NE // 2 + 1))
            v.wait_ge(gtT_ps, 1)
            V.tensor_copy(gtT, db[0:NE, 0:SEQ]).then_inc(fin_dve, 1)
            v.wait_ge(bd_ps, 1)
            v.wait_ge(tail_in, 32)
            for t in range(TT):
                for b in range(2):
                    h = slice(512 * b, 512 * b + 512)
                    ins = V.tensor_tensor(xh[:, t, h], accb[t][b][:, :], xh[:, t, h], ALU.add)
                ins.then_inc(fin_dve, 1)
                v.wait_ge(fin_dve, t + 2)
                ins = V.tensor_tensor_reduce(out=outb[:, t, :], in0=xh[:, t, :], in1=xh[:, t, :], scale=1.0, scalar=0.0,
                                             op0=ALU.mult, op1=ALU.add, accum_out=ssq3[:, t:t + 1])
            ins.then_inc(fin_dve, 1)
            v.wait_ge(fin_dve, TT + 2)
            V.tensor_scalar(rstd3, ssq3, 1.0 / D, NEG_EPS, ALU.mult, ALU.add).then_inc(ms3_ok, 1)
            v.wait_ge(rt3_ok, 1)
            V.reciprocal(rstd3, rstd3).then_inc(fin_dve, 1)
            v.wait_ge(fin_dve, TT + 3)
            for t in range(TT):
                V.scalar_tensor_tensor(outb[:, t, :], xh[:, t, :], rstd3[:, t:t + 1], gfin, ALU.mult, ALU.mult).then_inc(out_ok, 1)

        @block.tensor
        def _(pe):
            mm = nc.tensor.matmul
            pe.wait_ge(cst_in, 16)
            pe.wait_ge(vec_in, 16 * 11)
            for c in range(CC):
                nc.tensor.transpose(bank[7][:, c * NV:(c + 1) * NV], vrow[:, c * P:(c + 1) * P], ident[0:NV, 0:NV])
            nc.tensor.transpose(bank[7][:, CC * NV:CC * NV + NG], grow, ident[0:NG, 0:NG]).then_inc(vecT, 1)
            pe.wait_ge(un_ok, 3)
            for k in range(KD):
                ks = slice(k * P, (k + 1) * P)
                if k == KD - 1:
                    pe.wait_ge(vec_ok, 1)
                nc.tensor.transpose(bank[k][:, 0:META], metah[:, ks], ident[0:META, 0:META])
                for t in range(TT):
                    ins = nc.tensor.transpose(bank[k][:, META + t * P:META + (t + 1) * P], unat[:, t, ks], ident)
                ins.then_inc(uT_ps, 1)
            pe.wait_ge(uT_dve, KD // 2)
            pe.wait_ge(uT_act, KD // 2)

            def z_piece(p):
                pe.wait_ge(win_in[p], 32)
                if 2 <= p < 6:
                    pe.wait_ge(z_dve, p - 1)
                if p >= 6:
                    pe.wait_ge(z_act, CC + 2 * (p - 5))
                w = gu_ring[:, 0, p, :].rearrange("p (k b n) -> p k b n", k=KD, b=2)
                for b in range(2):
                    for k in range(KD):
                        ins = mm(bank[2 * (p % 2) + b][:, 0:T], w[:, k, b, :], uT[:, k, :], start=(k == 0), stop=(k == KD - 1))
                ins.then_inc(z_ps, 1)

            def lru_gates(c):
                pe.wait_ge(lu_ok, c + 1)
                if c:
                    pe.wait_ge(lg_act, 3 * c - 1)
                mm(bank[6][:, 0:T], bdiag[:, c, :], lu[:, c, :], start=True, stop=True)
                mm(bank[7][:, 0:T], bdiag[:, CC + c, :], lu[:, c, :], start=True, stop=True).then_inc(lg_ps, 1)

            for p in range(KD):
                z_piece(p)
            pe.wait_ge(yc_ok, CC)
            for c in range(CC):
                ins = mm(bank[4][:, 0:SEQ], ones, yc[:, c, :], start=(c == 0), stop=(c == CC - 1))
            ins.then_inc(mean_ps, 1)
            pe.wait_ge(lruw_in, 64)
            for c in range(CC):
                lru_gates(c)
            pe.wait_ge(sq2_ok, 1)
            for c in range(CC):
                ins = mm(bank[5][:, 0:SEQ], ones, lnsq[:, c, :], start=(c == 0), stop=(c == CC - 1))
            ins.then_inc(var_ps, 1)
            pe.wait_ge(z_act, CC + 2 * CC)
            for k in range(KD):
                if k % CC == 0:
                    pe.wait_ge(mix_ok, k // CC + 1)
                if k % 2 == 0:
                    pe.wait_ge(wout_in[k // 2], 16)
                for t in range(TT):
                    for b in range(2):
                        ins = mm(bank[2 * t + b][:, :], mixT[:, k, t * P:(t + 1) * P], dn_ring[:, k, 512 * b:512 * b + 512],
                                 start=(k == 0), stop=(k == KD - 1))
                        if k == KD - 1 and (t, b) != (TT - 1, 1):
                            ins.then_inc(h_ps, 1)
                if k == KD - 1:
                    ins.then_inc(h_ps, 1)
                elif k % 2:
                    ins.then_inc(wout_used, 1)
            for t in range(TT):
                pe.wait_ge(h_ok, 2 * t + 2)
                for b in range(2):
                    for k in range(4):
                        kk = 4 * b + k
                        ins = nc.tensor.transpose(bank[4 + 2 * t + b][:, k * P:(k + 1) * P], xh[:, t, kk * P:(kk + 1) * P], ident)
                    ins.then_inc(hT_ps, 1)
            pe.wait_ge(wr_ok, 1)
            for t in range(TT):
                pe.wait_ge(hT_ok, 2 * t + 2)
                for k in range(KD):
                    ins = mm(bank[0][:, NE * t:NE * (t + 1)], hT[:, t, k, :], wr[:, k, :], start=(k == 0), stop=(k == KD - 1))
            ins.then_inc(lg2_ps, 1)
            pe.wait_ge(mask_ok, 1)
            mm(bank[1][:, 0:NE], tri, mask[:, 0, :], start=True, stop=True)
            mm(bank[1][:, NE:2 * NE], ones, mask[:, 0, :], start=True, stop=False)
            mm(bank[1][:, NE:2 * NE], tri, mask[:, 1, :], start=False, stop=True).then_inc(pos_ps, 1)
            c9 = slice(0, CAND)
            pe.wait_ge(x_dve, 1)
            for t in range(TT):
                ins = mm(bank[2][c9, 0:1], mask3[:, t, :, :].rearrange("p b e -> p (b e)"), ones[:, 0:1], start=(t == 0), stop=(t == TT - 1))
            ins.then_inc(x_pe, 1)
            pe.wait_ge(x_dve, 2)
            mm(bank[2][c9, 1:2], cst[c9, C_TRI96:C_TRI96 + CAND], fx[c9, 0:1], start=True, stop=True).then_inc(x_pe, 1)
            for i in range(2):
                for t in range(TT):
                    ins = nc.tensor.transpose(bank[3][c9, i * SEQ + t * P:i * SEQ + (t + 1) * P], cand[i][:, t, :], ident)
            ins.then_inc(x_pe, 1)
            pe.wait_ge(x_dve, 5)
            for i in range(2):
                for t in range(TT):
                    at = 64 + 32 * i + XCOLS * t
                    mm(bank[2][:, at:at + XCOLS], candT[i][:, t * P:(t + 1) * P], sel96[c9, :], start=True, stop=True)
            mm(bank[2][c9, 128:128 + XCOLS], cst[c9, C_RR:C_RR + CAND], sel96[c9, :], start=True, stop=True)
            mm(bank[2][0:1, 160:160 + XCOLS], cst[c9, C_EID:C_EID + 1], sel96[c9, :], start=True, stop=True)
            mm(bank[2][0:1, 160 + XCOLS:161 + XCOLS], fx[c9, 0:1], ones[c9, 0:1], start=True, stop=True).then_inc(x_pe, 1)

            pe.wait_ge(q_ok, 1)
            for t in range(TT):
                for b in range(2):
                    ins = mm(accb[t][b][:, :], zeros[:, 0:P], zeros[:, P:P + 512], start=True, stop=True)
            ins.then_inc(acc_ps, 1)

            def gather(n, after):
                pe.wait_ge(oh_ok, after)
                for k in range(KD):
                    for t in range(TT):
                        ins = mm(db[:, k * SLOTS:(k + 1) * SLOTS], xn[:, t, k * P:(k + 1) * P], onehot[:, t, :],
                                 start=(t == 0), stop=(t == TT - 1))
                ins.then_inc(gath_ps, 1)

            gather(0, 1)
            pe.wait_ge(pool_step, bias_steps)

            def expert(n, s, loads):
                pe.wait_ge(xg_ok, n * 2 + 2)
                pe.wait_ge(gu_read, n + 1)
                for b in range(2):
                    for h in range(2):
                        mm(gub[b][64 * h:64 * h + 64, :], selb[0:CAND, :], biasp[:, 1024 * h + 512 * b:1024 * h + 512 * b + 512],
                           start=True, stop=False)
                for j in range(KD):
                    pe.wait_ge(gu_in[s][j], loads * 16)
                    for b in range(2):
                        for h in range(2):
                            ins = mm(gub[b][64 * h:64 * h + 64, :], xgT[:, j, :],
                                     gu_ring[:, s, j, 1024 * h + 512 * b:1024 * h + 512 * b + 512],
                                     start=False, stop=(j == KD - 1))
                    ins.then_inc(gu_used[s], 1)
                pe.wait_ge(oh_ok, n * 2 + 3)
                for t in range(TT):
                    ins = nc.tensor.transpose(tb[:, t * P:(t + 1) * P], wonehot[:, t, :], ident)
                ins.then_inc(gT_ps, 1)
                gather(n + 1, n * 2 + 3)
                pe.wait_ge(act_ok, n + 1)
                pe.wait_ge(gT_ok, n + 1)
                for c in range(4):
                    ins = nc.tensor.transpose(tb[:, c * P:(c + 1) * P], actv[:, c * P:(c + 1) * P], ident)
                ins.then_inc(aT_ps, 1)
                pe.wait_ge(aT_ok, n + 1)
                pe.wait_ge(xg_ok, n * 2 + 4)
                for k in range(KD):
                    if k % 2 == 0:
                        pe.wait_ge(dn_in[k // 2], n * 16 + 16)
                    at = (k % 4) * P + (k // 4) * SLOTS
                    for h in range(2):
                        ins = mm(db[64 * h:64 * h + 64, :], actT[:, at:at + SLOTS], dn_ring[:, k, 512 * h:512 * h + 512],
                                 start=(k == 0), stop=(k == KD - 1))
                    if k % 2 and k < KD - 1:
                        ins.then_inc(dn_used, 1)
                ins.then_inc(y_ps, 1)
                pe.wait_ge(y_ok, n + 1)
                for t in range(TT):
                    for h in range(2):
                        ins = mm(accb[t][h][:, :], gT[64 * h:64 * h + 64, t * P:(t + 1) * P], yv[64 * h:64 * h + 64, :],
                                 start=False, stop=True, skip_group_check=True)
                ins.then_inc(acc_ps, 1)

            with pe.Fori(0, NE // 2) as g:
                expert(g * 2, 1, g + 1)
                expert(g * 2 + 1, 0, g + 1)
            n_x = pe.value_load(qi[0:1, XCOLS:XCOLS + 1], min_val=0, max_val=XCOLS - 1)
            with pe.If(n_x > 0):
                with pe.Fori(0, n_x) as q:
                    expert(q + NE, 0, q + (NE // 2 + 1))
            for t in range(TT):
                ins = nc.tensor.transpose(db[0:NE, t * P:(t + 1) * P], gatet[:, t, 0:NE], ident)
            ins.then_inc(gtT_ps, 1)
            pe.wait_ge(fin_dve, 1)
            pe.wait_ge(tail_in, 32)
            for t in range(TT):
                for b in range(2):
                    ins = mm(accb[t][b][:, :], gtT[:, t * P:(t + 1) * P], bdn[:, 512 * b:512 * b + 512],
                             start=False, stop=True, skip_group_check=True)
            ins.then_inc(bd_ps, 1)


def kernel(**inputs):
    import numpy as _np
    import concourse.bacc as _bacc
    from concourse import mybir as _mybir
    from concourse.bass_utils import run_bass_kernel_spmd as _run

    nc = _bacc.Bacc("TRN2", target_bir_lowering=False, num_devices=1)
    names = ["x", "meta_tokens", "g_mix", "w_in", "conv_dw_w", "conv_dw_b", "conv_ln_g", "conv_ln_b",
             "lru_conv_w", "lru_conv_b", "lru_wa", "lru_ba", "lru_wx", "lru_bx", "lru_lambda", "w_out",
             "g_ffn", "w_router", "b_router", "w_gate_up", "b_gate_up", "w_down", "b_down", "g_final"]
    arrays, args = {}, []
    for name in names + ["shape_constants"]:
        a = constants() if name == "shape_constants" else _np.ascontiguousarray(inputs[name])
        arrays[f"in_{name}"] = a
        args.append(nc.dram_tensor(f"in_{name}", a.shape, _mybir.dt.from_np(a.dtype), kind="ExternalInput").ap())
    out = nc.dram_tensor("out_0", (1, SEQ, D), _mybir.dt.float32, kind="ExternalOutput").ap()
    build(nc, *args, out)
    r = _run(nc, [arrays], core_ids=[0])
    return r.results[0]["out_0"]
```

```python
import concourse.bass as bass
from concourse import mybir
from concourse.alu_op_type import AluOpType as ALU
from contextlib import ExitStack
import numpy as np

f32 = mybir.dt.float32
bf16 = mybir.dt.bfloat16
i32 = mybir.dt.int32
ACT = mybir.ActivationFunctionType
AX = mybir.AxisListType

P = 128
D = 1024
KD = D // P
META = 16
SEQ = 256
T = META + SEQ
TT = SEQ // P
CW = 512
CC = CW // P
TAPS = 31
LTAPS = 4
NE = 32
TOPK = 4
F2 = 2 * D
SLOTS = 64
EXTRA = SEQ // SLOTS - 1
CAND = EXTRA * NE
XCOLS = 16
ITEMS = NE + XCOLS
NEG_EPS, LN_EPS = 1e-6, 1e-5

V_CW, V_CB, V_LG, V_LB, V_LW, V_LCB, V_BA, V_BX, V_LAM = 0, 31, 32, 33, 34, 38, 39, 40, 41
NV = 42
BC = 256
NG = 2 * KD

C_ID, C_ONE, C_TRI, C_SLOT = 0, P, 2 * P, 3 * P
C_TRI96 = 4 * P
C_RR = C_TRI96 + CAND
C_THRB = C_RR + CAND
C_IOTA = C_THRB + P
C_EID = C_IOTA + XCOLS
C_THRC = C_EID + 1
C_COLS = C_THRC + 1


def constants():
    c = np.zeros((P, C_COLS), np.float32)
    r = np.arange(P)[:, None]
    c[:, C_ID:C_ID + P] = r == np.arange(P)
    c[:, C_ONE:C_ONE + P] = 1.0
    c[:, C_TRI:C_TRI + P] = r < np.arange(P)
    c[:, C_SLOT:C_SLOT + P] = np.arange(P) % SLOTS
    q = np.arange(CAND)
    c[:CAND, C_TRI96:C_TRI96 + CAND] = q[:, None] < q
    c[:CAND, C_RR:C_RR + CAND] = (q[:, None] % NE) == (q % NE)
    c[:CAND, C_THRB:C_THRB + P] = -SLOTS * (q[:, None] // NE + 1)
    c[:, C_IOTA:C_IOTA + XCOLS] = np.arange(XCOLS)
    c[:CAND, C_EID] = q % NE
    c[:CAND, C_THRC] = SLOTS * (q // NE + 1)
    return c


def build(nc, x, meta, g_mix, w_in, cdw, cdb, clg, clb, lcw, lcb, lwa, lba, lwx, lbx, lam,
          w_out, g_ffn, w_router, b_router, w_gu, b_gu, w_dn, b_dn, g_final, const, out):
    ctx = ExitStack()
    with ctx:
        def sb(name, cols, dt=f32):
            return ctx.enter_context(nc.sbuf_tensor(name, [P, cols], dt))

        def sem(name):
            return ctx.enter_context(nc.semaphore(name))

        gu_ring = ctx.enter_context(nc.sbuf_tensor("gu_ring", [P, 2, KD, F2], f32))
        dn_ring = ctx.enter_context(nc.sbuf_tensor("dn_ring", [P, KD, D], f32))
        xh = ctx.enter_context(nc.sbuf_tensor("xh", [P, TT, D], f32))
        reg2 = sb("reg2", KD * T)
        reg3 = sb("reg3", KD * SEQ)
        reg4 = sb("reg4", CC * 302 + T + CC * SEQ + SEQ)
        reg5 = sb("reg5", F2 // 2)
        cst = sb("cst", C_COLS)
        colv = sb("colv", CC * NV + NG)
        stage = sb("stage", BC)
        wr = ctx.enter_context(nc.sbuf_tensor("wr", [P, KD, NE], f32))
        tiny = sb("tiny", 112)

        ident = cst[:, C_ID:C_ID + P]
        ones = cst[:, C_ONE:C_ONE + P]
        tri = cst[:, C_TRI:C_TRI + P]
        slot_no = cst[:, C_SLOT:C_SLOT + P]

        uT = reg2[:, :].rearrange("p (k t) -> p k t", k=KD)
        unat = reg3[:, :].rearrange("p (t d) -> p t d", t=TT)
        mixT = reg3[:, :].rearrange("p (k t) -> p k t", k=KD)
        scr = gu_ring[:, 0, 0:4, :].rearrange("p a b -> p (a b)")
        o = 2 * F2
        rx = scr[:, o:o + CC * 275].rearrange("p (c t) -> p c t", c=CC)
        o += CC * 275
        lru = []
        for _ in range(5):
            lru.append(scr[:, o:o + CC * T].rearrange("p (c t) -> p c t", c=CC))
            o += CC * T
            if len(lru) == 2:
                o = 0
        rg, lu, ltau, li, lr = lru
        diag = gu_ring[:, 0, 0:2, :].rearrange("p a b -> p (a b)")[:, 0:TAPS * P].rearrange("p (k n) -> p k n", k=TAPS)
        metah = gu_ring[0:META, 1, KD - 1, 0:D]
        vrow = gu_ring[0:NV, 1, KD - 2, 0:CW]
        grow = gu_ring[0:NG, 1, KD - 2, CW:CW + P]
        o = 0
        gpad = reg4[:, o:o + CC * 302].rearrange("p (c t) -> p c t", c=CC)
        o += CC * 302
        sig = reg4[:, o:o + T]
        o += T
        yc = reg4[:, o:o + CC * SEQ].rearrange("p (c t) -> p c t", c=CC)
        o += CC * SEQ
        acc2 = reg4[:, o:o + SEQ]
        lnsq = gpad[:, :, 0:SEQ]
        bdiag = reg3[:, KD * SEQ // 2:].rearrange("p (c n) -> p c n", c=2 * CC)

        xn = reg2[:, 0:TT * D].rearrange("p (t d) -> p t d", t=TT)
        hT = reg3[:, :].rearrange("p (t k n) -> p t k n", t=TT, k=KD)
        biasp = reg5[0:3 * NE, :].bitcast(bf16)
        o = 0
        xgT = reg3[:, 0:512].rearrange("p (k s) -> p k s", k=KD)
        actv = reg3[:, 512:1024]
        xglu = reg3[:, 1024:1536]
        sigm = reg3[:, 1536:2048]
        lin = reg4[:, 0:512]
        actT = reg4[:, 512:1024]
        yv = reg4[:, 1024:1536]
        gT = reg4[:, 1536:1792]
        onehot = reg4[:, 1792:1920].rearrange("p (t s) -> p t s", t=TT)
        wonehot = reg4[:, 1920:2176].rearrange("p (t s) -> p t s", t=TT)
        tabs = reg4[:, 2176:]
        o = 0

        def small(n):
            nonlocal o
            o += n
            return tabs[:, o - n:o]
        post = small(TT * ITEMS).rearrange("p (t e) -> p t e", t=TT)
        gatet = small(TT * ITEMS).rearrange("p (t e) -> p t e", t=TT)
        selt = small(ITEMS)
        selb = small(SLOTS // 2).bitcast(bf16)
        qi = small(XCOLS + 1).bitcast(i32)
        rt = reg4[:, 0:1024]
        o = 0

        def rsmall(n):
            nonlocal o
            o += n
            return rt[:, o - n:o]

        def two(a, n):
            return a.rearrange("p (t e) -> p t e", t=TT)
        lg = two(rsmall(TT * NE), NE)
        mx = two(rsmall(TT * 8), 8)
        gt = two(rsmall(TT * NE), NE)
        eq = two(rsmall(TT * NE), NE)
        ceq = two(rsmall(TT * NE), NE)
        ex = two(rsmall(TT * NE), NE)
        cnt = two(rsmall(TT), 1)
        den = two(rsmall(TT), 1)
        mask = two(rsmall(TT * NE), NE)
        brow = tiny[:, 48:48 + NE]
        zeros = reg3[:, 1536:2048].bitcast(bf16)
        fx = tiny[:, 36:38]
        sel96 = tiny[0:CAND, 80:80 + XCOLS]
        sel32 = tiny[0:NE, 96:96 + XCOLS]
        postT = stage[0:NE, :]
        gateT = wr[0:NE, :, :].rearrange("p k e -> p (k e)")
        ssq = tiny[:, 0:3]
        rstd = tiny[:, 3:6]
        sp4 = tiny[:, 8:12]
        spt = [tiny[:, 12 + 4 * i:16 + 4 * i] for i in range(4)]
        ssq2, rstd2 = tiny[:, 28:30], tiny[:, 30:32]
        ssq3, rstd3 = tiny[:, 32:34], tiny[:, 34:36]
        gfin = gu_ring[:, 1, 0, 0:D]
        bdn = gu_ring[0:NE, 1, 1, 0:D]
        outb = gu_ring[:, 1, 2, :].rearrange("p (t d) -> p t d", t=TT)

        bank = [ctx.enter_context(nc.psum_tensor(f"bank{i}", [P, 512], f32)) for i in range(8)]
        accb = [[bank[0], bank[1]], [bank[2], bank[3]]]
        gub = [bank[4], bank[5]]
        tb, db = bank[6], bank[7]

        def col(v, c):
            return colv[:, c * NV + v:c * NV + v + 1]

        def gcol(k):
            return colv[:, CC * NV + k:CC * NV + k + 1]

        x_in, meta_in, vec_in, cst_in = sem("x_in"), sem("meta_in"), sem("vec_in"), sem("cst_in")
        lruw_in, route_in = sem("lruw_in"), sem("route_in")
        win_in = [sem(f"win_in{p}") for p in range(KD)]
        wout_in = [sem(f"wout_in{j}") for j in range(4)]
        gu_in = [[sem(f"gu_in{s}_{j}") for j in range(KD)] for s in range(2)]
        dn_in = [sem(f"dn_in{j}") for j in range(4)]
        gu_used = [sem("gu_used0"), sem("gu_used1")]
        dn_used = sem("dn_used")
        wout_used = sem("wout_used")
        dv = sem("dve_step")
        pool_step, bias_in, bd_zero = sem("pool_step"), sem("bias_in"), sem("bd_zero")
        vecT, vec_ok = sem("vecT"), sem("vec_ok")
        diag_ok, c3_ps, c3_ok = sem("diag_ok"), sem("c3_ps"), sem("c3_ok")
        ss_act, ms_ok, rt_ok, un_ok = sem("ss_act"), sem("ms_ok"), sem("rt_ok"), sem("un_ok")
        uT_ps, uT_dve, uT_act = sem("uT_ps"), sem("uT_dve"), sem("uT_act")
        z_ps, z_dve, z_act = sem("z_ps"), sem("z_dve"), sem("z_act")
        sp_act, sp_dve = sem("sp_act"), sem("sp_dve")
        lu_ok, lg_ps, lg_act = sem("lu_ok"), sem("lg_ps"), sem("lg_act")
        gelu_ok, sq_ok, rinv_ok = sem("gelu_ok"), sem("sq_ok"), sem("rinv_ok")
        yc_ok, mean_ps, xc_ok, sq2_ok, var_ps = (sem(n) for n in ("yc_ok", "mean_ps", "xc_ok", "sq2_ok", "var_ps"))
        lnv_ok, lns_ok, yn_ok, lsig_ok = sem("lnv_ok"), sem("lns_ok"), sem("yn_ok"), sem("lsig_ok")
        mix_ok, h_ps, h_ok = sem("mix_ok"), sem("h_ps"), sem("h_ok")
        ss2_ok, ms2_ok, rt2_ok = sem("ss2_ok"), sem("ms2_ok"), sem("rt2_ok")
        hT_ps, hT_ok, wr_ok, lg2_ps = sem("hT_ps"), sem("hT_ok"), sem("wr_ok"), sem("lg2_ps")
        ex_in, ex_ok, mask_ok, pos_ps = sem("ex_in"), sem("ex_ok"), sem("mask_ok"), sem("pos_ps")
        x_dve, x_pe, q_ok = sem("x_dve"), sem("x_pe"), sem("q_ok")
        oh_ok, gath_ps, xg_ok = sem("oh_ok"), sem("gath_ps"), sem("xg_ok")
        glu_ok, gu_read, sg_ok, act_ok = sem("glu_ok"), sem("gu_read"), sem("sg_ok"), sem("act_ok")
        gT_ps, gT_ok, aT_ps, aT_ok = sem("gT_ps"), sem("gT_ok"), sem("aT_ps"), sem("aT_ok")
        y_ps, y_ok, acc_ps = sem("y_ps"), sem("y_ok"), sem("acc_ps")
        tail_in, gfin_in, fin_dve, fin_ss, bd_ps, ms3_ok, rt3_ok, out_ok, out_done = (
            sem(n) for n in ("tail_in", "gfin_in", "fin_dve", "fin_ss", "bd_ps", "ms3_ok", "rt3_ok", "out_ok", "out_done"))

        w_in_v = w_in[0].rearrange("(k p) (b c n) -> p k b c n", p=P, b=4, c=CC)
        w_out_v = w_out[0].rearrange("(k p) n -> p k n", p=P)
        gu_v = w_gu[0].rearrange("e (k p) n -> p e k n", p=P)
        dn_v = w_dn[0].rearrange("e (k p) n -> p e k n", p=P)

        block = ctx.enter_context(nc.Block())

        @block.sync
        def _(sp):
            for t in range(TT):
                sp.dma_start(xh[:, t, :], x[0, t * P:(t + 1) * P, :]).then_inc(x_in, 16)
            sp.dma_start(cst[:, :], const).then_inc(cst_in, 16)
            for p in range(KD):
                piece = gu_ring[:, 0, p, :].rearrange("p (k b n) -> p k b n", k=KD, b=2)
                for b in range(2):
                    sp.dma_start(piece[:, :, b, :], w_in_v[:, :, 2 * (p // CC) + b, p % CC, :]).then_inc(win_in[p], 16)
            for j in range(4):
                sp.dma_start(dn_ring[:, 2 * j:2 * j + 2, :], w_out_v[:, 2 * j:2 * j + 2, :]).then_inc(wout_in[j], 16)

            def gu_load(s, e, done):
                for j in range(KD):
                    sp.wait_ge(gu_used[s], done * KD + (j + 1))
                    sp.dma_start(gu_ring[:, s, j, :], gu_v[:, e, j, :]).then_inc(gu_in[s][j], 16)

            def dn_load(e, done):
                for j in range(4):
                    if j < 3:
                        sp.wait_ge(dn_used, done * 3 + (j + 1))
                    else:
                        sp.wait_ge(y_ps, done + 1)
                    sp.dma_start(dn_ring[:, 2 * j:2 * j + 2, :], dn_v[:, e, 2 * j:2 * j + 2, :]).then_inc(dn_in[j], 16)

            sp.wait_ge(vecT, 1)
            sp.wait_ge(uT_ps, KD)
            for j in range(KD):
                sp.dma_start(gu_ring[:, 1, j, :], gu_v[:, 0, j, :]).then_inc(gu_in[1][j], 16)
            for j in list(range(4, KD)) + list(range(4)):
                if j >= 4:
                    sp.wait_ge(z_ps, j + 1)
                else:
                    sp.wait_ge(mix_ok, 2)
                sp.dma_start(gu_ring[:, 0, j, :], gu_v[:, 1, j, :]).then_inc(gu_in[0][j], 16)
            for j in range(4):
                if j < 3:
                    sp.wait_ge(wout_used, j + 1)
                else:
                    sp.wait_ge(h_ps, 2 * TT)
                sp.dma_start(dn_ring[:, 2 * j:2 * j + 2, :], dn_v[:, 0, 2 * j:2 * j + 2, :]).then_inc(dn_in[j], 16)
            dn_load(1, 0)
            with sp.Fori(1, NE // 2 - 1) as g:
                gu_load(1, g * 2, g - 1)
                dn_load(g * 2, g * 2 - 1)
                gu_load(0, g * 2 + 1, g - 1)
                dn_load(g * 2 + 1, g * 2)
            gu_load(1, NE - 2, NE // 2 - 2)
            dn_load(NE - 2, NE - 3)
            gu_load(0, NE - 1, NE // 2 - 2)
            sp.wait_ge(gu_used[1], NE // 2 * KD)
            sp.dma_start(bdn, b_dn[0]).then_inc(tail_in, 16)
            sp.dma_start(gfin, g_final.partition_broadcast(P)).then_inc(gfin_in, 16)
            dn_load(NE - 1, NE - 2)
            sp.wait_ge(q_ok, 1)
            n_x = sp.value_load(qi[0:1, XCOLS:XCOLS + 1], min_val=0, max_val=XCOLS - 1)
            with sp.If(n_x > 0):
                with sp.Fori(0, n_x) as q:
                    e = sp.value_load(qi[0:1, bass.ds(q, 1)], min_val=0, max_val=NE - 1)
                    gu_load(0, e, q + (NE // 2 - 1))
                    dn_load(e, q + (NE - 1))
            for t in range(TT):
                for b in range(2):
                    h = slice(512 * b, 512 * b + 512)
                    sp.wait_ge(out_ok, 2 * t + b + 1)
                    sp.dma_start(out[0, t * P:(t + 1) * P, h], outb[:, t, h]).then_inc(out_done, 16)
            sp.wait_ge(out_done, 32 * TT)

        @block.gpsimd
        def _(pool):
            pool.dma_start(wr[:, :, :], w_router[0].rearrange("(k p) e -> p k e", p=P)).then_inc(route_in, 16)
            pool.dma_start(brow, b_router[0].partition_broadcast(P)).then_inc(route_in, 16)
            pool.wait_ge(uT_ps, KD)
            nc.gpsimd.memset(bdiag[:, :, :], 0.0).then_inc(bd_zero, 1)
            pool.wait_ge(bd_zero, 1)
            for w, src in enumerate((lwa, lwx)):
                s4 = src[0].rearrange("(c h) i j -> h i c j", h=2)
                for h in range(2):
                    pool.dma_start(bdiag[64 * h:64 * h + 64, CC * w:CC * (w + 1), 64 * h:64 * h + 64], s4[h]).then_inc(lruw_in, 16)
            steps = 0
            for c in range(F2 // BC):
                at = slice(BC * c, BC * c + BC)
                for part in range(3):
                    pool.dma_start(stage[part * NE:(part + 1) * NE, :], b_gu[0, :, at]).then_inc(bias_in, 16)
                pool.wait_ge(bias_in, 48 * (c + 1))
                for part in range(3):
                    for r0 in range(part, 3) if part else (0,):
                        rows_ = slice(r0 * NE, (r0 + 1) * NE) if part else slice(0, CAND)
                        nc.gpsimd.tensor_copy(biasp[rows_, at], stage[rows_, :]).then_inc(pool_step, 1)
                        steps += 1
                        pool.wait_ge(pool_step, steps)
                    if part < 2:
                        rows_ = slice(2 * NE, 3 * NE) if part else slice(0, CAND)
                        nc.gpsimd.tensor_tensor(stage[rows_, :], stage[rows_, :], biasp[rows_, at], ALU.subtract).then_inc(pool_step, 1)
                        steps += 1
                        pool.wait_ge(pool_step, steps)

        bias_steps = F2 // BC * 6

        @block.scalar
        def _(act):
            act.dma_start(metah, meta).then_inc(meta_in, 16)
            rows = [(V_CW, TAPS, cdw[0]), (V_CB, 1, cdb), (V_LG, 1, clg), (V_LB, 1, clb), (V_LW, LTAPS, lcw[0]),
                    (V_LCB, 1, lcb), (V_BA, 1, lba), (V_BX, 1, lbx), (V_LAM, 1, lam)]
            for r, n, src in rows:
                act.dma_start(vrow[r:r + n, :], src).then_inc(vec_in, 16)
            act.dma_start(grow[0:KD, :], g_mix[0].rearrange("(k n) -> k n", k=KD)).then_inc(vec_in, 16)
            act.dma_start(grow[KD:2 * KD, :], g_ffn[0].rearrange("(k n) -> k n", k=KD)).then_inc(vec_in, 16)
            act.wait_ge(x_in, 32)
            nc.scalar.activation(unat[:, 1, :], xh[:, 1, :], ACT.Square, accum_out=ssq[:, 1:2]).then_inc(ss_act, 1)
            act.wait_ge(ms_ok, 1)
            nc.scalar.activation(rstd, rstd, ACT.Sqrt).then_inc(rt_ok, 1)
            act.wait_ge(sp_dve, 1)
            nc.scalar.activation(spt[1], spt[0], ACT.Exp, scale=-1.0).then_inc(sp_act, 1)
            act.wait_ge(vec_ok, 1)
            for k in range(1, KD, 2):
                act.wait_ge(uT_ps, k + 1)
                nc.scalar.activation(uT[:, k, :], bank[k][:, 0:T], ACT.Copy, scale=gcol(k)).then_inc(uT_act, 1)
            def diagonals(lo, hi):
                for k in range(lo, hi):
                    nc.scalar.activation(diag[:, k, :], ident, ACT.Copy, scale=col(V_CW + k, CC - 1)).then_inc(diag_ok, 1)

            for c in range(CC):
                act.wait_ge(z_ps, c + 1)
                if c:
                    act.wait_ge(z_dve, c)
                nc.scalar.activation(sig, bank[2 * (c % 2) + 1][:, 0:T], ACT.Sigmoid).then_inc(z_act, 1)
                if c == 1:
                    diagonals(0, TAPS // 2)
                if c == 2:
                    diagonals(TAPS // 2, TAPS)

            def lru_copies(c):
                act.wait_ge(z_ps, CC + c + 1)
                b = 2 * (c % 2)
                nc.scalar.activation(rx[:, c, 3:3 + T], bank[b][:, 0:T], ACT.Copy).then_inc(z_act, 1)
                nc.scalar.activation(rg[:, c, :], bank[b + 1][:, 0:T], ACT.Copy).then_inc(z_act, 1)

            def lru_gate(c):
                act.wait_ge(lg_ps, c + 1)
                nc.scalar.activation(ltau[:, c, :], bank[6][:, 0:T], ACT.Sigmoid, bias=col(V_BA, c)).then_inc(lg_act, 1)
                nc.scalar.activation(li[:, c, :], bank[7][:, 0:T], ACT.Sigmoid, bias=col(V_BX, c)).then_inc(lg_act, 1)
                act.wait_ge(lg_act, 3 * c + 1)
                nc.scalar.activation(ltau[:, c, :], ltau[:, c, :], ACT.Tanh, scale=sp4[:, c:c + 1]).then_inc(lg_act, 1)

            def lru_sqrt(c):
                act.wait_ge(rinv_ok, c + 2)
                act.wait_ge(lg_act, 3 * (c + 2))
                nc.scalar.activation(ltau[:, c:c + 2, :], ltau[:, c:c + 2, :], ACT.Sqrt, scale=4.0).then_inc(sq_ok, 1)

            act.wait_ge(c3_ps, 1)
            nc.scalar.activation(yc[:, CC - 1, :], bank[4][:, 0:SEQ], ACT.Identity, bias=col(V_CB, CC - 1)).then_inc(c3_ok, 1)
            act.wait_ge(sp_dve, 2)
            lru_copies(0)
            act.wait_ge(xc_ok, 1)
            nc.scalar.activation(lnsq, yc[:, :, :], ACT.Square).then_inc(sq2_ok, 1)
            lru_copies(1)
            act.wait_ge(lnv_ok, 1)
            nc.scalar.activation(acc2, acc2, ACT.Sqrt).then_inc(lns_ok, 1)
            lru_gate(0)
            act.wait_ge(yn_ok, 1)
            for c in range(CC):
                nc.scalar.activation(lnsq[:, c, :], yc[:, c, :], ACT.Sigmoid, bias=col(V_LB, c), scale=col(V_LG, c)).then_inc(lsig_ok, 1)
            lru_copies(2)
            lru_gate(1)
            lru_sqrt(0)
            lru_copies(3)
            act.wait_ge(z_act, CC + 2 * CC)
            nc.scalar.activation(rg[:, :, :], rg[:, :, :], ACT.Gelu_apprx_tanh).then_inc(gelu_ok, 1)
            lru_gate(2)
            lru_gate(3)
            lru_sqrt(2)
            for t in range(TT):
                act.wait_ge(h_ok, 2 * t + 2)
                nc.scalar.activation(xn[:, t, :], xh[:, t, :], ACT.Square, accum_out=ssq2[:, t:t + 1]).then_inc(ss2_ok, 1)
            act.wait_ge(ms2_ok, 1)
            nc.scalar.activation(rstd2, rstd2, ACT.Sqrt).then_inc(rt2_ok, 1)
            for t in range(TT):
                act.wait_ge(hT_ps, 2 * t + 2)
                for b in range(2):
                    nc.scalar.activation(hT[:, t, 4 * b:4 * b + 4, :], bank[4 + 2 * t + b][:, :].rearrange("p (k n) -> p k n", k=4), ACT.Copy).then_inc(hT_ok, 1)
            act.wait_ge(ex_in, 1)
            nc.scalar.activation(ex[:, :, :], ex[:, :, :], ACT.Exp).then_inc(ex_ok, 1)

            def expert(n):
                act.wait_ge(gT_ps, n + 1)
                act.wait_ge(acc_ps, n + 1)
                nc.scalar.activation(gT, tb[:, 0:SEQ], ACT.Copy).then_inc(gT_ok, 1)
                act.wait_ge(glu_ok, n + 1)
                nc.scalar.activation(sigm, xglu, ACT.Sigmoid, scale=1.702).then_inc(sg_ok, 1)
                act.wait_ge(aT_ps, n + 1)
                nc.scalar.activation(actT, tb[:, :], ACT.Copy).then_inc(aT_ok, 1)
                act.wait_ge(y_ps, n + 1)
                nc.scalar.activation(yv, db[:, :], ACT.Copy).then_inc(y_ok, 1)

            with act.Fori(0, NE) as n:
                expert(n)
            act.wait_ge(q_ok, 1)
            n_x = act.value_load(qi[0:1, XCOLS:XCOLS + 1], min_val=0, max_val=XCOLS - 1)
            with act.If(n_x > 0):
                with act.Fori(0, n_x) as q:
                    expert(q + NE)
            nc.scalar.activation(tiny[:, 38:39], tiny[:, 39:40], ACT.Sqrt).then_inc(fin_ss, 1)
            for t in range(TT):
                act.wait_ge(fin_dve, 2 * t + 2)
                nc.scalar.activation(outb[:, t, :], xh[:, t, :], ACT.Square, accum_out=ssq3[:, t:t + 1]).then_inc(fin_ss, 1)
                act.wait_ge(ms3_ok, t + 1)
                nc.scalar.activation(rstd3[:, t:t + 1], rstd3[:, t:t + 1], ACT.Sqrt).then_inc(rt3_ok, 1)

        @block.vector
        def _(v):
            step = [0]

            def link(ins):
                step[0] += 1
                ins.then_inc(dv, 1)
                v.wait_ge(dv, step[0])

            def mark(ins):
                step[0] += 1
                ins.then_inc(dv, 1)
                return step[0]

            V = nc.vector
            link(V.memset(ssq[:, 2:3], 1.0))
            link(V.memset(tiny[:, 39:40], 1.0))
            link(V.memset(gpad[:, :, 0:TAPS - 1], 0.0))
            v.wait_ge(meta_in, 16)
            link(V.tensor_tensor_reduce(out=reg2[0:META, 0:D], in0=metah, in1=metah, scale=1.0, scalar=0.0,
                                        op0=ALU.mult, op1=ALU.add, accum_out=ssq[0:META, 2:3]))
            v.wait_ge(x_in, 32)
            link(V.tensor_tensor_reduce(out=unat[:, 0, :], in0=xh[:, 0, :], in1=xh[:, 0, :], scale=1.0, scalar=0.0,
                                        op0=ALU.mult, op1=ALU.add, accum_out=ssq[:, 0:1]))
            v.wait_ge(ss_act, 1)
            V.tensor_scalar(rstd, ssq, 1.0 / D, NEG_EPS, ALU.mult, ALU.add).then_inc(ms_ok, 1)
            v.wait_ge(rt_ok, 1)
            link(V.reciprocal(rstd, rstd))
            V.tensor_scalar(metah, metah, rstd[0:META, 2:3], None, ALU.mult).then_inc(un_ok, 1)
            for t in range(TT):
                V.tensor_scalar(unat[:, t, :], xh[:, t, :], rstd[:, t:t + 1], None, ALU.mult).then_inc(un_ok, 1)
            v.wait_ge(vecT, 1)
            V.tensor_copy(colv[:, :], bank[7][:, 0:CC * NV + NG]).then_inc(vec_ok, 1)
            v.wait_ge(vec_ok, 1)
            lamc = colv[:, 0:CC * NV].rearrange("p (c n) -> p c n", c=CC)[:, :, V_LAM]
            link(V.tensor_scalar(spt[3], lamc, -1.0, 0.0, ALU.mult, ALU.max))
            link(V.tensor_scalar(spt[2], lamc, 0.0, None, ALU.max))
            V.tensor_tensor(spt[0], spt[3], spt[2], ALU.add).then_inc(sp_dve, 1)
            for k in range(0, KD, 2):
                v.wait_ge(uT_ps, k + 1)
                V.tensor_scalar(uT[:, k, :], bank[k][:, 0:T], gcol(k), None, ALU.mult).then_inc(uT_dve, 1)
            v.wait_ge(sp_act, 1)
            link(V.tensor_scalar(spt[2], spt[1], 2.0, None, ALU.add))
            link(V.reciprocal(spt[2], spt[2]))
            link(V.tensor_tensor(spt[1], spt[1], spt[2], ALU.mult))
            link(V.tensor_tensor(spt[2], spt[1], spt[1], ALU.mult))
            link(V.memset(spt[0], 1.0 / 17))
            for d in (15, 13, 11, 9, 7, 5, 3, 1):
                link(V.tensor_tensor(spt[0], spt[0], spt[2], ALU.mult))
                link(V.tensor_scalar(spt[0], spt[0], 1.0 / d, None, ALU.add))
            link(V.tensor_tensor(spt[0], spt[0], spt[1], ALU.mult))
            link(V.scalar_tensor_tensor(spt[0], spt[0], 2.0, spt[3], ALU.mult, ALU.add))
            V.tensor_scalar(sp4, spt[0], 4.0, None, ALU.mult).then_inc(sp_dve, 1)

            def glu(c):
                v.wait_ge(z_act, c + 1)
                V.tensor_tensor(gpad[:, c, TAPS - 1:TAPS - 1 + T], bank[2 * (c % 2)][:, 0:T], sig, ALU.mult).then_inc(z_dve, 1)

            glu(0)
            between = {(0, 17): 1, (1, 4): 2, (1, 22): 3}
            for c in range(CC - 1):
                v.wait_ge(z_dve, c + 1)
                two_sums = [yc[:, c, :], acc2]
                last = [0, 0]
                for k in range(TAPS):
                    src = gpad[:, c, META + k:META + k + SEQ]
                    a = two_sums[k % 2]
                    if k == 0:
                        last[0] = mark(V.tensor_scalar(a, src, col(V_CW, c), col(V_CB, c), ALU.mult, ALU.add))
                    elif k == 1:
                        last[1] = mark(V.tensor_scalar(a, src, col(V_CW + 1, c), None, ALU.mult))
                    else:
                        v.wait_ge(dv, last[k % 2])
                        last[k % 2] = mark(V.scalar_tensor_tensor(a, src, col(V_CW + k, c), a, ALU.mult, ALU.add))
                    if (c, k) in between:
                        glu(between[c, k])
                v.wait_ge(dv, step[0])
                V.tensor_tensor(yc[:, c, :], yc[:, c, :], acc2, ALU.add).then_inc(yc_ok, 1)
                v.wait_ge(yc_ok, c + 1)

            def lru_conv(c):
                v.wait_ge(z_act, CC + 2 * c + 2)
                link(V.tensor_scalar(lu[:, c, :], rx[:, c, 0:T], col(V_LW, c), col(V_LCB, c), ALU.mult, ALU.add))
                for k in range(1, LTAPS):
                    ins = V.scalar_tensor_tensor(lu[:, c, :], rx[:, c, k:k + T], col(V_LW + k, c), lu[:, c, :], ALU.mult, ALU.add)
                    if k < LTAPS - 1:
                        link(ins)
                    else:
                        ins.then_inc(lu_ok, 1)

            def lru_in(c):
                v.wait_ge(lg_act, 3 * c + 3)
                link(V.tensor_scalar(lr[:, c, :], ltau[:, c, :], 1.0, None, ALU.add))
                V.reciprocal(lr[:, c, :], lr[:, c, :]).then_inc(rinv_ok, 1)
                v.wait_ge(lu_ok, c + 1)
                link(V.tensor_tensor(li[:, c, :], li[:, c, :], lu[:, c, :], ALU.mult))

            def lru_scan(c0):
                cs = slice(c0, c0 + 2)
                v.wait_ge(sq_ok, c0 // 2 + 1)
                v.wait_ge(rinv_ok, c0 + 2)
                link(V.tensor_tensor(ltau[:, cs, :], ltau[:, cs, :], lr[:, cs, :], ALU.mult))
                link(V.memset(ltau[:, cs, 0:1], 1.0))
                link(V.tensor_tensor(li[:, cs, :], li[:, cs, :], ltau[:, cs, :], ALU.mult))
                link(V.tensor_scalar(lr[:, cs, :], lr[:, cs, :], 2.0, -1.0, ALU.mult, ALU.add))
                for c in range(c0, c0 + 2):
                    link(V.tensor_tensor_scan(lu[:, c, :], lr[:, c, :], li[:, c, :], 0.0, ALU.mult, ALU.add))

            v.wait_ge(z_ps, CC)
            link(V.memset(rx[:, :, 0:3], 0.0))
            lru_conv(0)
            v.wait_ge(mean_ps, 1)
            mean = bank[4][:, 0:SEQ].unsqueeze(1).to_broadcast([P, CC, SEQ])
            V.scalar_tensor_tensor(yc[:, :, :], mean, -1.0 / CW, yc[:, :, :], ALU.mult, ALU.add).then_inc(xc_ok, 1)
            lru_conv(1)
            v.wait_ge(var_ps, 1)
            V.tensor_scalar(acc2, bank[5][:, 0:SEQ], 1.0 / CW, LN_EPS, ALU.mult, ALU.add).then_inc(lnv_ok, 1)
            v.wait_ge(lns_ok, 1)
            link(V.reciprocal(acc2, acc2))
            V.tensor_tensor(yc[:, :, :], yc[:, :, :], acc2.unsqueeze(1).to_broadcast([P, CC, SEQ]), ALU.mult).then_inc(yn_ok, 1)
            lru_in(0)
            v.wait_ge(lsig_ok, CC)
            for c in range(CC):
                link(V.tensor_scalar(yc[:, c, :], yc[:, c, :], col(V_LG, c), col(V_LB, c), ALU.mult, ALU.add))
            V.tensor_tensor(mixT[:, 0:CC, :], yc[:, :, :], lnsq, ALU.mult).then_inc(mix_ok, 1)
            lru_conv(2)
            lru_in(1)
            lru_scan(0)
            lru_conv(3)
            lru_in(2)
            lru_in(3)
            lru_scan(2)
            v.wait_ge(gelu_ok, 1)
            V.tensor_tensor(mixT[:, CC:, :], lu[:, :, META:], rg[:, :, META:], ALU.mult).then_inc(mix_ok, 1)
            def one_hot(n):
                for t in range(TT):
                    ins = V.tensor_scalar(onehot[:, t, :], slot_no[:, 0:SLOTS], post[:, t, bass.ds(n, 1)], None, ALU.is_equal)
                ins.then_inc(oh_ok, 1)

            v.wait_ge(route_in, 32)
            for k in range(KD):
                ins = V.tensor_scalar(wr[:, k, :], wr[:, k, :], gcol(KD + k), None, ALU.mult)
                if k < KD - 1:
                    link(ins)
            ins.then_inc(wr_ok, 1)
            for t in range(TT):
                for b in range(2):
                    v.wait_ge(h_ps, 2 * t + b + 1)
                    V.tensor_tensor(xh[:, t, 512 * b:512 * b + 512], bank[2 * t + b][:, :], xh[:, t, 512 * b:512 * b + 512], ALU.add).then_inc(h_ok, 1)
            v.wait_ge(ss2_ok, TT)
            V.tensor_scalar(rstd2, ssq2, 1.0 / D, NEG_EPS, ALU.mult, ALU.add).then_inc(ms2_ok, 1)
            v.wait_ge(rt2_ok, 1)
            link(V.reciprocal(rstd2, rstd2))
            v.wait_ge(lg2_ps, 1)
            for t in range(TT):
                link(V.scalar_tensor_tensor(lg[:, t, :], bank[0][:, NE * t:NE * (t + 1)], rstd2[:, t:t + 1], brow, ALU.mult, ALU.add))
            for t in range(TT):
                link(V.max(mx[:, t, :], lg[:, t, :]))
            V.tensor_tensor(ex[:, :, :], lg[:, :, :], mx[:, :, 0:1].to_broadcast([P, TT, NE]), ALU.subtract).then_inc(ex_in, 1)
            v4 = mx[:, :, TOPK - 1:TOPK].to_broadcast([P, TT, NE])
            link(V.tensor_tensor(gt[:, :, :], lg[:, :, :], v4, ALU.is_gt))
            link(V.tensor_tensor(eq[:, :, :], lg[:, :, :], v4, ALU.is_equal))
            link(V.tensor_reduce(cnt[:, :, 0], gt[:, :, :], axis=AX.X, op=ALU.add))
            for t in range(TT):
                link(V.tensor_tensor_scan(ceq[:, t, :], ones[:, 0:NE], eq[:, t, :], 0.0, ALU.mult, ALU.add))
            link(V.tensor_tensor(ceq[:, :, :], ceq[:, :, :], cnt[:, :, 0:1].to_broadcast([P, TT, NE]), ALU.add))
            link(V.scalar_tensor_tensor(eq[:, :, :], ceq[:, :, :], float(TOPK), eq[:, :, :], ALU.is_le, ALU.mult))
            V.tensor_tensor(mask[:, :, :], gt[:, :, :], eq[:, :, :], ALU.add).then_inc(mask_ok, 1)
            v.wait_ge(ex_ok, 1)
            v.wait_ge(mask_ok, 1)
            link(V.tensor_tensor(ex[:, :, :], ex[:, :, :], mask[:, :, :], ALU.mult))
            link(V.tensor_reduce(den[:, :, 0], ex[:, :, :], axis=AX.X, op=ALU.add))
            link(V.reciprocal(den[:, :, :], den[:, :, :]))
            link(V.tensor_tensor(gatet[:, :, 0:NE], ex[:, :, :], den[:, :, 0:1].to_broadcast([P, TT, NE]), ALU.mult))
            for t in range(TT):
                link(V.tensor_scalar(xn[:, t, :], xh[:, t, :], rstd2[:, t:t + 1], None, ALU.mult))
            v.wait_ge(pos_ps, 1)
            pos_v = bank[1][:, 0:TT * NE].rearrange("p (t e) -> p t e", t=TT)
            link(V.scalar_tensor_tensor(post[:, :, 0:NE], pos_v, 1.0, mask[:, :, :], ALU.add, ALU.mult))
            link(V.tensor_scalar(post[:, :, 0:NE], post[:, :, 0:NE], -1.0, None, ALU.add))
            one_hot(0)
            for b in range(3):
                link(V.tensor_copy(selt[b * NE:(b + 1) * NE, 0:NE], ident[b * NE:(b + 1) * NE, b * NE:(b + 1) * NE]))

            v.wait_ge(x_pe, 1)
            c9 = slice(0, CAND)
            V.tensor_scalar(fx[c9, 0:1], bank[2][c9, 0:1], cst[c9, C_THRC:C_THRC + 1], None, ALU.is_gt).then_inc(x_dve, 1)
            V.memset(zeros, 0.0).then_inc(gu_read, 1)

            def gathered(n):
                v.wait_ge(gath_ps, n + 1)
                V.tensor_tensor(xgT[:, :, :], db[:, :].rearrange("p (k s) -> p k s", k=KD),
                                colv[:, CC * NV + KD:].unsqueeze(2).to_broadcast([P, KD, SLOTS]), ALU.mult).then_inc(xg_ok, 1)
                V.tensor_scalar(selb[0:CAND, :], ones[0:CAND, 0:SLOTS], selt[0:CAND, bass.ds(n, 1)], None, ALU.mult).then_inc(xg_ok, 1)

            gathered(0)
            v.wait_ge(x_pe, 2)
            link(V.tensor_copy(fx[c9, 1:2], bank[2][c9, 1:2]))
            V.tensor_scalar(sel96, cst[c9, C_IOTA:C_IOTA + XCOLS], fx[c9, 1:2], fx[c9, 0:1], ALU.is_equal, ALU.mult).then_inc(x_dve, 1)
            base = step[0]

            def expert(n, s, use):
                one_hot(n + 1)
                for t in range(TT):
                    ins = V.tensor_scalar(wonehot[:, t, :], slot_no, post[:, t, bass.ds(n, 1)], gatet[:, t, bass.ds(n, 1)], ALU.is_equal, ALU.mult)
                ins.then_inc(oh_ok, 1)
                v.wait_ge(gu_used[s], use * KD)
                for b in range(2):
                    glu_v = gub[b][:, :].rearrange("p (n two) -> p n two", two=2)
                    h = slice(256 * b, 256 * b + 256)
                    ins = V.tensor_scalar(xglu[:, h], glu_v[:, :, 0], 7.0, None, ALU.min)
                ins.then_inc(glu_ok, 1)
                for b in range(2):
                    glu_v = gub[b][:, :].rearrange("p (n two) -> p n two", two=2)
                    h = slice(256 * b, 256 * b + 256)
                    ins = V.tensor_scalar(lin[:, h], glu_v[:, :, 1], 7.0, -7.0, ALU.min, ALU.max)
                ins.then_inc(gu_read, 1)
                v.wait_ge(gu_read, n + 2)
                v.wait_ge(glu_ok, n + 1)
                V.scalar_tensor_tensor(lin, lin, 1.0, xglu, ALU.add, ALU.mult).then_inc(dv, 1)
                v.wait_ge(dv, n + (base + 1))
                v.wait_ge(sg_ok, n + 1)
                V.tensor_tensor(actv, lin, sigm, ALU.mult).then_inc(act_ok, 1)
                gathered(n + 1)

            expert(0, 1, 1)
            v.wait_ge(x_pe, 3)
            V.tensor_copy(postT, tb[0:NE, 0:SEQ])
            V.tensor_copy(gateT, tb[0:NE, SEQ:2 * SEQ])
            V.tensor_copy(sel32, db[0:NE, 0:XCOLS])
            V.tensor_copy(selt[c9, NE:], db[c9, XCOLS:2 * XCOLS])
            V.tensor_copy(qi[0:1, :], db[0:1, 2 * XCOLS:3 * XCOLS + 1]).then_inc(x_dve, 1)
            expert(1, 0, 1)
            v.wait_ge(x_pe, 4)
            for i, table in enumerate((post, gatet)):
                src = db[:, 2 * XCOLS * i:2 * XCOLS * (i + 1)].rearrange("p (t q) -> p t q", t=TT)
                ins = V.tensor_copy(table[:, :, NE:], src)
            ins.then_inc(q_ok, 1)
            v.wait_ge(q_ok, 1)
            with v.Fori(1, NE // 2) as g:
                expert(g * 2, 1, g + 1)
                expert(g * 2 + 1, 0, g + 1)
            v.wait_ge(q_ok, 1)
            n_x = v.value_load(qi[0:1, XCOLS:XCOLS + 1], min_val=0, max_val=XCOLS - 1)
            with v.If(n_x > 0):
                with v.Fori(0, n_x) as q:
                    expert(q + NE, 0, q + (NE // 2 + 1))
            v.wait_ge(bd_ps, 1)
            for t in range(TT):
                for b in range(2):
                    h = slice(512 * b, 512 * b + 512)
                    V.tensor_tensor(xh[:, t, h], accb[t][b][:, :], xh[:, t, h], ALU.add).then_inc(fin_dve, 1)
            v.wait_ge(gfin_in, 16)
            for t in range(TT):
                ts = slice(t, t + 1)
                v.wait_ge(fin_ss, t + 2)
                V.tensor_scalar(rstd3[:, ts], ssq3[:, ts], 1.0 / D, NEG_EPS, ALU.mult, ALU.add).then_inc(ms3_ok, 1)
                v.wait_ge(rt3_ok, t + 1)
                V.reciprocal(rstd3[:, ts], rstd3[:, ts]).then_inc(fin_dve, 1)
                v.wait_ge(fin_dve, 2 * TT + t + 1)
                for b in range(2):
                    h = slice(512 * b, 512 * b + 512)
                    V.scalar_tensor_tensor(outb[:, t, h], xh[:, t, h], rstd3[:, ts], gfin[:, h], ALU.mult, ALU.mult).then_inc(out_ok, 1)

        @block.tensor
        def _(pe):
            mm = nc.tensor.matmul
            pe.wait_ge(cst_in, 16)
            pe.wait_ge(vec_in, 16 * 11)
            for c in range(CC):
                nc.tensor.transpose(bank[7][:, c * NV:(c + 1) * NV], vrow[:, c * P:(c + 1) * P], ident[0:NV, 0:NV])
            nc.tensor.transpose(bank[7][:, CC * NV:CC * NV + NG], grow, ident[0:NG, 0:NG]).then_inc(vecT, 1)
            pe.wait_ge(un_ok, 3)
            for k in range(KD):
                ks = slice(k * P, (k + 1) * P)
                if k == KD - 1:
                    pe.wait_ge(vec_ok, 1)
                nc.tensor.transpose(bank[k][:, 0:META], metah[:, ks], ident[0:META, 0:META])
                for t in range(TT):
                    ins = nc.tensor.transpose(bank[k][:, META + t * P:META + (t + 1) * P], unat[:, t, ks], ident)
                ins.then_inc(uT_ps, 1)
            pe.wait_ge(uT_dve, KD // 2)
            pe.wait_ge(uT_act, KD // 2)

            def z_piece(p):
                pe.wait_ge(win_in[p], 32)
                if 2 <= p < 6:
                    pe.wait_ge(z_dve, p - 1)
                if p >= 6:
                    pe.wait_ge(z_act, CC + 2 * (p - 5))
                w = gu_ring[:, 0, p, :].rearrange("p (k b n) -> p k b n", k=KD, b=2)
                for b in range(2):
                    for k in range(KD):
                        ins = mm(bank[2 * (p % 2) + b][:, 0:T], w[:, k, b, :], uT[:, k, :], start=(k == 0), stop=(k == KD - 1))
                ins.then_inc(z_ps, 1)

            def lru_gates(c):
                pe.wait_ge(lu_ok, c + 1)
                if c:
                    pe.wait_ge(lg_act, 3 * c - 1)
                mm(bank[6][:, 0:T], bdiag[:, c, :], lu[:, c, :], start=True, stop=True)
                mm(bank[7][:, 0:T], bdiag[:, CC + c, :], lu[:, c, :], start=True, stop=True).then_inc(lg_ps, 1)

            for p in range(CC):
                z_piece(p)
            pe.wait_ge(z_dve, CC)
            for k in range(TAPS):
                if k == 0:
                    pe.wait_ge(diag_ok, TAPS // 2)
                if k == TAPS // 2:
                    pe.wait_ge(diag_ok, TAPS)
                ins = mm(bank[4][:, 0:SEQ], diag[:, k, :], gpad[:, CC - 1, META + k:META + k + SEQ],
                         start=(k == 0), stop=(k == TAPS - 1))
            ins.then_inc(c3_ps, 1)
            z_piece(CC)
            pe.wait_ge(yc_ok, CC - 1)
            pe.wait_ge(c3_ok, 1)
            for c in range(CC):
                ins = mm(bank[4][:, 0:SEQ], ones, yc[:, c, :], start=(c == 0), stop=(c == CC - 1))
            ins.then_inc(mean_ps, 1)
            z_piece(CC + 1)
            pe.wait_ge(sq2_ok, 1)
            for c in range(CC):
                ins = mm(bank[5][:, 0:SEQ], ones, lnsq[:, c, :], start=(c == 0), stop=(c == CC - 1))
            ins.then_inc(var_ps, 1)
            pe.wait_ge(lruw_in, 64)
            lru_gates(0)
            z_piece(CC + 2)
            lru_gates(1)
            z_piece(CC + 3)
            lru_gates(2)

            def out_proj(t, b, k):
                return mm(bank[2 * t + b][:, :], mixT[:, k, t * P:(t + 1) * P], dn_ring[:, k, 512 * b:512 * b + 512],
                          start=(k == 0), stop=(k == KD - 1))

            pe.wait_ge(z_act, CC + 2 * CC)
            pe.wait_ge(mix_ok, 1)
            for k in range(CC):
                if k % 2 == 0:
                    pe.wait_ge(wout_in[k // 2], 16)
                for t in range(TT):
                    for b in range(2):
                        ins = out_proj(t, b, k)
                if k % 2:
                    ins.then_inc(wout_used, 1)
                if k == 1:
                    lru_gates(3)
            pe.wait_ge(mix_ok, 2)
            pe.wait_ge(wout_in[2], 16)
            pe.wait_ge(wout_in[3], 16)
            for t in range(TT):
                for k in range(CC, KD):
                    for b in range(2):
                        ins = out_proj(t, b, k)
                        if k == KD - 1:
                            ins.then_inc(h_ps, 1)
                    if k == CC + 1 and t == TT - 1:
                        ins.then_inc(wout_used, 1)
            for t in range(TT):
                pe.wait_ge(h_ok, 2 * t + 2)
                for b in range(2):
                    for k in range(4):
                        kk = 4 * b + k
                        ins = nc.tensor.transpose(bank[4 + 2 * t + b][:, k * P:(k + 1) * P], xh[:, t, kk * P:(kk + 1) * P], ident)
                    ins.then_inc(hT_ps, 1)
            pe.wait_ge(wr_ok, 1)
            for t in range(TT):
                pe.wait_ge(hT_ok, 2 * t + 2)
                for k in range(KD):
                    ins = mm(bank[0][:, NE * t:NE * (t + 1)], hT[:, t, k, :], wr[:, k, :], start=(k == 0), stop=(k == KD - 1))
            ins.then_inc(lg2_ps, 1)
            pe.wait_ge(mask_ok, 1)
            mm(bank[1][:, 0:NE], tri, mask[:, 0, :], start=True, stop=True)
            mm(bank[1][:, NE:2 * NE], ones, mask[:, 0, :], start=True, stop=False)
            mm(bank[1][:, NE:2 * NE], tri, mask[:, 1, :], start=False, stop=True).then_inc(pos_ps, 1)
            for b in range(EXTRA):
                for t in range(TT):
                    ins = mm(bank[2][b * NE:(b + 1) * NE, 0:1], mask[:, t, :], ones[:, 0:1], start=(t == 0), stop=(t == TT - 1))
            ins.then_inc(x_pe, 1)

            def gather(n, after):
                pe.wait_ge(oh_ok, after)
                for k in range(KD):
                    for t in range(TT):
                        ins = mm(db[:, k * SLOTS:(k + 1) * SLOTS], xn[:, t, k * P:(k + 1) * P], onehot[:, t, :],
                                 start=(t == 0), stop=(t == TT - 1))
                ins.then_inc(gath_ps, 1)

            gather(0, 1)
            c9 = slice(0, CAND)
            pe.wait_ge(x_dve, 1)
            mm(bank[2][c9, 1:2], cst[c9, C_TRI96:C_TRI96 + CAND], fx[c9, 0:1], start=True, stop=True).then_inc(x_pe, 1)
            pe.wait_ge(pool_step, bias_steps)

            def expert(n, s, loads, before_turn=None, before_down=None):
                pe.wait_ge(xg_ok, n * 2 + 2)
                pe.wait_ge(gu_read, n + 1)
                for b in range(2):
                    for h in range(2):
                        mm(gub[b][64 * h:64 * h + 64, :], selb[0:CAND, :], biasp[:, 1024 * h + 512 * b:1024 * h + 512 * b + 512],
                           start=True, stop=False)
                for j in range(KD):
                    pe.wait_ge(gu_in[s][j], loads * 16)
                    for b in range(2):
                        for h in range(2):
                            ins = mm(gub[b][64 * h:64 * h + 64, :], xgT[:, j, :],
                                     gu_ring[:, s, j, 1024 * h + 512 * b:1024 * h + 512 * b + 512],
                                     start=False, stop=(j == KD - 1))
                    ins.then_inc(gu_used[s], 1)
                if before_turn:
                    before_turn()
                pe.wait_ge(oh_ok, n * 2 + 3)
                for t in range(TT):
                    ins = nc.tensor.transpose(tb[:, t * P:(t + 1) * P], wonehot[:, t, :], ident)
                ins.then_inc(gT_ps, 1)
                gather(n + 1, n * 2 + 3)
                pe.wait_ge(act_ok, n + 1)
                pe.wait_ge(gT_ok, n + 1)
                for c in range(4):
                    ins = nc.tensor.transpose(tb[:, c * P:(c + 1) * P], actv[:, c * P:(c + 1) * P], ident)
                ins.then_inc(aT_ps, 1)
                if before_down:
                    before_down()
                pe.wait_ge(aT_ok, n + 1)
                pe.wait_ge(xg_ok, n * 2 + 4)
                for k in range(KD):
                    if k % 2 == 0:
                        pe.wait_ge(dn_in[k // 2], n * 16 + 16)
                    at = (k % 4) * P + (k // 4) * SLOTS
                    for h in range(2):
                        ins = mm(db[64 * h:64 * h + 64, :], actT[:, at:at + SLOTS], dn_ring[:, k, 512 * h:512 * h + 512],
                                 start=(k == 0), stop=(k == KD - 1))
                    if k % 2 and k < KD - 1:
                        ins.then_inc(dn_used, 1)
                ins.then_inc(y_ps, 1)
                pe.wait_ge(y_ok, n + 1)
                for t in range(TT):
                    for h in range(2):
                        ins = mm(accb[t][h][:, :], gT[64 * h:64 * h + 64, t * P:(t + 1) * P], yv[64 * h:64 * h + 64, :],
                                 start=False, stop=True, skip_group_check=True)
                ins.then_inc(acc_ps, 1)

            def zero_sums():
                pe.wait_ge(gu_read, 1)
                pe.wait_ge(x_dve, 2)
                for t in range(TT):
                    for b in range(2):
                        ins = mm(accb[t][b][:, :], zeros[:, 0:P], zeros[:, P:P + 512], start=True, stop=True)
                ins.then_inc(acc_ps, 1)

            def wait_list():
                pe.wait_ge(x_dve, 3)

            def add_b_down():
                pe.wait_ge(tail_in, 16)
                for t in range(TT):
                    for b in range(2):
                        mm(accb[t][b][:, :], gateT[:, t * P:(t + 1) * P], bdn[:, 512 * b:512 * b + 512],
                           start=False, stop=True, skip_group_check=True)

            zero_sums()
            expert(0, 1, 1)
            for i, table in enumerate((post, gatet)):
                for t in range(TT):
                    nc.tensor.transpose(tb[0:NE, i * SEQ + t * P:i * SEQ + (t + 1) * P], table[:, t, 0:NE], ident)
            mm(db[0:NE, 0:XCOLS], cst[c9, C_RR:C_RR + NE], sel96, start=True, stop=True)
            mm(db[c9, XCOLS:2 * XCOLS], cst[c9, C_RR:C_RR + CAND], sel96, start=True, stop=True)
            mm(db[0:1, 2 * XCOLS:3 * XCOLS], cst[c9, C_EID:C_EID + 1], sel96, start=True, stop=True)
            mm(db[0:1, 3 * XCOLS:3 * XCOLS + 1], fx[c9, 0:1], ones[c9, 0:1], start=True, stop=True).then_inc(x_pe, 1)
            expert(1, 0, 1, before_turn=wait_list)
            for i, table in enumerate((postT, gateT)):
                for t in range(TT):
                    o_ = db[:, (2 * i + t) * XCOLS:(2 * i + t + 1) * XCOLS]
                    ins = mm(o_, table[:, t * P:(t + 1) * P], sel32, start=True, stop=(i == 1))
                    if i == 0:
                        ins = mm(o_, cst[c9, C_THRB:C_THRB + P], sel96, start=False, stop=True)
            ins.then_inc(x_pe, 1)
            pe.wait_ge(q_ok, 1)
            with pe.Fori(1, NE // 2 - 1) as g:
                expert(g * 2, 1, g + 1)
                expert(g * 2 + 1, 0, g + 1)
            expert(NE - 2, 1, NE // 2)
            expert(NE - 1, 0, NE // 2, before_down=add_b_down)
            n_x = pe.value_load(qi[0:1, XCOLS:XCOLS + 1], min_val=0, max_val=XCOLS - 1)
            with pe.If(n_x > 0):
                with pe.Fori(0, n_x) as q:
                    expert(q + NE, 0, q + (NE // 2 + 1))
            nc.tensor.matmul(db[:, 0:1], ones, ones[:, 0:1], start=True, stop=True).then_inc(bd_ps, 1)


def kernel(**inputs):
    import numpy as _np
    import concourse.bacc as _bacc
    from concourse import mybir as _mybir
    from concourse.bass_utils import run_bass_kernel_spmd as _run

    nc = _bacc.Bacc("TRN2", target_bir_lowering=False, num_devices=1)
    names = ["x", "meta_tokens", "g_mix", "w_in", "conv_dw_w", "conv_dw_b", "conv_ln_g", "conv_ln_b",
             "lru_conv_w", "lru_conv_b", "lru_wa", "lru_ba", "lru_wx", "lru_bx", "lru_lambda", "w_out",
             "g_ffn", "w_router", "b_router", "w_gate_up", "b_gate_up", "w_down", "b_down", "g_final"]
    arrays, args = {}, []
    for name in names + ["shape_constants"]:
        a = constants() if name == "shape_constants" else _np.ascontiguousarray(inputs[name])
        arrays[f"in_{name}"] = a
        args.append(nc.dram_tensor(f"in_{name}", a.shape, _mybir.dt.from_np(a.dtype), kind="ExternalInput").ap())
    out = nc.dram_tensor("out_0", (1, SEQ, D), _mybir.dt.float32, kind="ExternalOutput").ap()
    build(nc, *args, out)
    r = _run(nc, [arrays], core_ids=[0])
    return r.results[0]["out_0"]
```

```python
import concourse.bass as bass
from concourse import mybir
from concourse.alu_op_type import AluOpType as ALU
from contextlib import ExitStack
import numpy as np

f32 = mybir.dt.float32
bf16 = mybir.dt.bfloat16
i32 = mybir.dt.int32
ACT = mybir.ActivationFunctionType
AX = mybir.AxisListType

P = 128
D = 1024
KD = D // P
META = 16
SEQ = 256
T = META + SEQ
TT = SEQ // P
CW = 512
CC = CW // P
TAPS = 31
LTAPS = 4
NE = 32
TOPK = 4
F2 = 2 * D
SLOTS = 64
EXTRA = SEQ // SLOTS - 1
CAND = EXTRA * NE
XCOLS = 16
ITEMS = NE + XCOLS
TURN = 10
NEG_EPS, LN_EPS = 1e-6, 1e-5

V_CW, V_CB, V_LG, V_LB, V_LW, V_LCB, V_BA, V_BX, V_LAM = 0, 31, 32, 33, 34, 38, 39, 40, 41
NV = 42
BC = 256
NG = 2 * KD

C_ID, C_ONE, C_TRI, C_SLOT = 0, P, 2 * P, 3 * P
C_TRI96 = 4 * P
C_RR = C_TRI96 + CAND
C_THRB = C_RR + CAND
C_IOTA = C_THRB + P
C_EID = C_IOTA + XCOLS
C_THRC = C_EID + 1
C_COLS = C_THRC + 1


def constants():
    c = np.zeros((P, C_COLS), np.float32)
    r = np.arange(P)[:, None]
    c[:, C_ID:C_ID + P] = r == np.arange(P)
    c[:, C_ONE:C_ONE + P] = 1.0
    c[:, C_TRI:C_TRI + P] = r < np.arange(P)
    c[:, C_SLOT:C_SLOT + P] = np.arange(P) % SLOTS + 1
    q = np.arange(CAND)
    c[:CAND, C_TRI96:C_TRI96 + CAND] = q[:, None] < q
    c[:CAND, C_RR:C_RR + CAND] = (q[:, None] % NE) == (q % NE)
    c[:CAND, C_THRB:C_THRB + P] = -SLOTS * (q[:, None] // NE + 1)
    c[:, C_IOTA:C_IOTA + XCOLS] = np.arange(XCOLS)
    c[:CAND, C_EID] = q % NE
    c[:CAND, C_THRC] = SLOTS * (q // NE + 1)
    return c


def build(nc, x, meta, g_mix, w_in, cdw, cdb, clg, clb, lcw, lcb, lwa, lba, lwx, lbx, lam,
          w_out, g_ffn, w_router, b_router, w_gu, b_gu, w_dn, b_dn, g_final, const, out):
    ctx = ExitStack()
    with ctx:
        def sb(name, cols, dt=f32):
            return ctx.enter_context(nc.sbuf_tensor(name, [P, cols], dt))

        def sem(name):
            return ctx.enter_context(nc.semaphore(name))

        gu_ring = ctx.enter_context(nc.sbuf_tensor("gu_ring", [P, 2, KD, F2], f32))
        dn_ring = ctx.enter_context(nc.sbuf_tensor("dn_ring", [P, KD, D], f32))
        xh = ctx.enter_context(nc.sbuf_tensor("xh", [P, TT, D], f32))
        reg2 = sb("reg2", KD * T)
        reg3 = sb("reg3", KD * SEQ)
        reg4 = sb("reg4", CC * 302 + T + CC * SEQ + SEQ)
        reg5 = sb("reg5", F2 // 2)
        cst = sb("cst", C_COLS)
        colv = sb("colv", CC * NV + NG)
        stage = ctx.enter_context(nc.sbuf_tensor("stage", [P, 2, BC], f32))
        wr = ctx.enter_context(nc.sbuf_tensor("wr", [P, KD, NE], f32))
        tiny = sb("tiny", 112)

        ident = cst[:, C_ID:C_ID + P]
        ones = cst[:, C_ONE:C_ONE + P]
        tri = cst[:, C_TRI:C_TRI + P]
        slot_no = cst[:, C_SLOT:C_SLOT + P]

        uT = reg2[:, :].rearrange("p (k t) -> p k t", k=KD)
        unat = reg3[:, :].rearrange("p (t d) -> p t d", t=TT)
        mixT = reg3[:, :].rearrange("p (k t) -> p k t", k=KD)
        scr = gu_ring[:, 0, 0:4, :].rearrange("p a b -> p (a b)")
        o = 2 * F2
        rx = scr[:, o:o + CC * 275].rearrange("p (c t) -> p c t", c=CC)
        o += CC * 275
        lru = []
        for _ in range(5):
            lru.append(scr[:, o:o + CC * T].rearrange("p (c t) -> p c t", c=CC))
            o += CC * T
            if len(lru) == 2:
                o = 0
        rg, lu, ltau, li, lr = lru
        diag = gu_ring[:, 0, 0:2, :].rearrange("p a b -> p (a b)")[:, 0:TAPS * P].rearrange("p (k n) -> p k n", k=TAPS)
        metah = gu_ring[0:META, 1, KD - 1, 0:D]
        vrow = gu_ring[0:NV, 1, KD - 2, 0:CW]
        grow = gu_ring[0:NG, 1, KD - 2, CW:CW + P]
        o = 0
        gpad = reg4[:, o:o + CC * 302].rearrange("p (c t) -> p c t", c=CC)
        o += CC * 302
        sig = reg4[:, o:o + T]
        o += T
        yc = reg4[:, o:o + CC * SEQ].rearrange("p (c t) -> p c t", c=CC)
        o += CC * SEQ
        acc2 = reg4[:, o:o + SEQ]
        lnsq = gpad[:, :, 0:SEQ]
        bdiag = reg3[:, KD * SEQ // 2:].rearrange("p (c n) -> p c n", c=2 * CC)

        xn = reg2[:, 0:TT * D].rearrange("p (t d) -> p t d", t=TT)
        hT = reg3[:, :].rearrange("p (t k n) -> p t k n", t=TT, k=KD)
        biasp = reg5[0:3 * NE, :].bitcast(bf16)
        o = 0
        xgT = reg3[:, 0:512].rearrange("p (k s) -> p k s", k=KD)
        actv = reg3[:, 512:1024]
        xglu = reg3[:, 1024:1536]
        sigm = reg3[:, 1536:2048]
        lin = reg4[:, 0:512]
        actT = reg4[:, 512:1024]
        yv = reg4[:, 1024:1536]
        gT = reg4[:, 1536:1792]
        onehot = reg4[:, 1792:1920].rearrange("p (t s) -> p t s", t=TT)
        wonehot = reg4[:, 1920:2176].rearrange("p (t s) -> p t s", t=TT)
        tabs = reg4[:, 2176:]
        o = 0

        def small(n):
            nonlocal o
            o += n
            return tabs[:, o - n:o]
        post = small(TT * ITEMS).rearrange("p (t e) -> p t e", t=TT)
        gatet = small(TT * ITEMS).rearrange("p (t e) -> p t e", t=TT)
        selt = small(ITEMS)
        selb = small(SLOTS // 2).bitcast(bf16)
        qi = small(XCOLS + 1).bitcast(i32)
        rt = reg4[:, 0:1024]
        o = 0

        def rsmall(n):
            nonlocal o
            o += n
            return rt[:, o - n:o]

        def two(a, n):
            return a.rearrange("p (t e) -> p t e", t=TT)
        lg = two(rsmall(TT * NE), NE)
        mx = two(rsmall(TT * 8), 8)
        gt = two(rsmall(TT * NE), NE)
        eq = two(rsmall(TT * NE), NE)
        ceq = two(rsmall(TT * NE), NE)
        ex = two(rsmall(TT * NE), NE)
        cnt = two(rsmall(TT), 1)
        den = two(rsmall(TT), 1)
        mask = two(rsmall(TT * NE), NE)
        brow = tiny[:, 48:48 + NE]
        lgT = reg4[0:NE, 1024:1024 + SEQ]
        fx = tiny[:, 36:38]
        sel96 = tiny[0:CAND, 80:80 + XCOLS]
        sel32 = tiny[0:NE, 96:96 + XCOLS]
        postT = stage[0:NE, 0, :]
        gateT = wr[0:NE, :, :].rearrange("p k e -> p (k e)")
        ssq = tiny[:, 0:3]
        rstd = tiny[:, 3:6]
        sp4 = tiny[:, 8:12]
        spt = [tiny[:, 12 + 4 * i:16 + 4 * i] for i in range(4)]
        ssq2, rstd2 = tiny[:, 28:30], tiny[:, 30:32]
        ssq3, rstd3 = tiny[:, 40:44], tiny[:, 44:46]
        gfin = gu_ring[:, 1, 0, 0:D]
        bdn = gu_ring[0:NE, 1, 1, 0:D]
        outb = gu_ring[:, 1, 2, :].rearrange("p (t d) -> p t d", t=TT)

        bank = [ctx.enter_context(nc.psum_tensor(f"bank{i}", [P, 512], f32)) for i in range(8)]
        accb = [[bank[0], bank[1]], [bank[2], bank[3]]]
        gub = [bank[4], bank[5]]
        tb, db = bank[6], bank[7]

        def col(v, c):
            return colv[:, c * NV + v:c * NV + v + 1]

        def gcol(k):
            return colv[:, CC * NV + k:CC * NV + k + 1]

        x_in, meta_in, vec_in, cst_in = sem("x_in"), sem("meta_in"), sem("vec_in"), sem("cst_in")
        vec_in_pool = sem("vec_in_pool")
        lruw_in, route_in = sem("lruw_in"), sem("route_in")
        win_in = [sem(f"win_in{p}") for p in range(KD)]
        wout_in = [sem(f"wout_in{j}") for j in range(4)]
        gu_in = [[sem(f"gu_in{s}_{j}") for j in range(KD)] for s in range(2)]
        dn_in = [sem(f"dn_in{j}") for j in range(4)]
        gu_used = [sem("gu_used0"), sem("gu_used1")]
        dn_used = sem("dn_used")
        wout_used = sem("wout_used")
        dv = sem("dve_step")
        pool_step, bd_zero = sem("pool_step"), sem("bd_zero")
        bias_in = [sem("bias_in0"), sem("bias_in1")]
        vecT, vec_ok = sem("vecT"), sem("vec_ok")
        diag_ok, c3_ps, c3_ok = sem("diag_ok"), sem("c3_ps"), sem("c3_ok")
        rinv0_ok, ms_ok, rt_ok, un_ok = sem("rinv0_ok"), sem("ms_ok"), sem("rt_ok"), sem("un_ok")
        uT_ps, uT_dve, uT_act = sem("uT_ps"), sem("uT_dve"), sem("uT_act")
        z_ps, z_dve, z_act = sem("z_ps"), sem("z_dve"), sem("z_act")
        sp_act, sp_dve = sem("sp_act"), sem("sp_dve")
        lu_ok, lg_ps, lg_act = sem("lu_ok"), sem("lg_ps"), sem("lg_act")
        gelu_ok, sq_ok, rinv_ok = sem("gelu_ok"), sem("sq_ok"), sem("rinv_ok")
        yc_ok, mean_ps, xc_ok, sq2_ok, var_ps = (sem(n) for n in ("yc_ok", "mean_ps", "xc_ok", "sq2_ok", "var_ps"))
        lnv_ok, lns_ok, yn_ok, lsig_ok = sem("lnv_ok"), sem("lns_ok"), sem("yn_ok"), sem("lsig_ok")
        mix_ok, h_ps, h_ok = sem("mix_ok"), sem("h_ps"), sem("h_ok")
        ss2_ok, ms2_ok, rt2_ok = sem("ss2_ok"), sem("ms2_ok"), sem("rt2_ok")
        hT_ps, hT_ok, wr_ok, lg2_ps = sem("hT_ps"), sem("hT_ok"), sem("wr_ok"), sem("lg2_ps")
        lgT_ps, lgT_ok, rinv2_ok, xn_ok = sem("lgT_ps"), sem("lgT_ok"), sem("rinv2_ok"), sem("xn_ok")
        ex_in, ex_ok, mask_ok, pos_ps = sem("ex_in"), sem("ex_ok"), sem("mask_ok"), sem("pos_ps")
        x_dve, x_pe, q_ok = sem("x_dve"), sem("x_pe"), sem("q_ok")
        oh_ok, gath_ps, xg_ok = sem("oh_ok"), sem("gath_ps"), sem("xg_ok")
        glu_ok, gu_read, sg_ok, act_ok = sem("glu_ok"), sem("gu_read"), sem("sg_ok"), sem("act_ok")
        gT_ps, gT_ok, aT_ps, aT_ok = sem("gT_ps"), sem("gT_ok"), sem("aT_ps"), sem("aT_ok")
        y_ps, y_ok, acc_ps = sem("y_ps"), sem("y_ok"), sem("acc_ps")
        tail_in, gfin_in, fin_dve, fin_ss, bd_ps, ms3_ok, rt3_ok, out_ok, out_done = (
            sem(n) for n in ("tail_in", "gfin_in", "fin_dve", "fin_ss", "bd_ps", "ms3_ok", "rt3_ok", "out_ok", "out_done"))

        w_in_v = w_in[0].rearrange("(k p) (b c n) -> p k b c n", p=P, b=4, c=CC)
        w_out_v = w_out[0].rearrange("(k p) n -> p k n", p=P)
        gu_v = w_gu[0].rearrange("e (k p) n -> p e k n", p=P)
        dn_v = w_dn[0].rearrange("e (k p) n -> p e k n", p=P)

        vec_rows = [(V_CW, TAPS, cdw[0]), (V_CB, 1, cdb), (V_LG, 1, clg), (V_LB, 1, clb), (V_LW, LTAPS, lcw[0]),
                    (V_LCB, 1, lcb), (V_BA, 1, lba), (V_BX, 1, lbx), (V_LAM, 1, lam)]

        block = ctx.enter_context(nc.Block())

        @block.sync
        def _(sp):
            for t in range(TT):
                sp.dma_start(xh[:, t, :], x[0, t * P:(t + 1) * P, :]).then_inc(x_in, 16)
            sp.dma_start(cst[:, :], const).then_inc(cst_in, 16)
            for r, n, src in vec_rows[0:4]:
                sp.dma_start(vrow[r:r + n, :], src).then_inc(vec_in, 16)
            for p in range(KD):
                piece = gu_ring[:, 0, p, :].rearrange("p (k b n) -> p k b n", k=KD, b=2)
                for b in range(2):
                    sp.dma_start(piece[:, :, b, :], w_in_v[:, :, 2 * (p // CC) + b, p % CC, :]).then_inc(win_in[p], 16)
            for j in range(4):
                sp.dma_start(dn_ring[:, 2 * j:2 * j + 2, :], w_out_v[:, 2 * j:2 * j + 2, :]).then_inc(wout_in[j], 16)

            def gu_load(s, e, done):
                for j in range(KD):
                    sp.wait_ge(gu_used[s], done * KD + (j + 1))
                    sp.dma_start(gu_ring[:, s, j, :], gu_v[:, e, j, :]).then_inc(gu_in[s][j], 16)

            def dn_load(e, done):
                for j in range(4):
                    if j < 3:
                        sp.wait_ge(dn_used, done * 3 + (j + 1))
                    else:
                        sp.wait_ge(y_ps, done + 1)
                    sp.dma_start(dn_ring[:, 2 * j:2 * j + 2, :], dn_v[:, e, 2 * j:2 * j + 2, :]).then_inc(dn_in[j], 16)

            sp.wait_ge(vecT, 1)
            sp.wait_ge(uT_ps, KD)
            for j in range(KD):
                sp.dma_start(gu_ring[:, 1, j, :], gu_v[:, 0, j, :]).then_inc(gu_in[1][j], 16)
            for j in list(range(4, KD)) + list(range(4)):
                if j >= 4:
                    sp.wait_ge(z_ps, j + 1)
                else:
                    sp.wait_ge(mix_ok, 3)
                    sp.wait_ge(wout_used, 3)
                sp.dma_start(gu_ring[:, 0, j, :], gu_v[:, 1, j, :]).then_inc(gu_in[0][j], 16)
            for j in range(4):
                if j < 3:
                    sp.wait_ge(wout_used, j + 1)
                else:
                    sp.wait_ge(h_ps, 2 * TT)
                sp.dma_start(dn_ring[:, 2 * j:2 * j + 2, :], dn_v[:, 0, 2 * j:2 * j + 2, :]).then_inc(dn_in[j], 16)
            with sp.Fori(1, TURN) as g:
                gu_load(1, g * 2, g - 1)
                dn_load(g * 2 - 1, g * 2 - 2)
                gu_load(0, g * 2 + 1, g - 1)
                dn_load(g * 2, g * 2 - 1)
            gu_load(1, TURN * 2, TURN - 1)
            dn_load(TURN * 2 - 1, TURN * 2 - 2)
            dn_load(TURN * 2, TURN * 2 - 1)
            gu_load(0, TURN * 2 + 1, TURN - 1)
            dn_load(TURN * 2 + 1, TURN * 2)
            with sp.Fori(TURN + 1, NE // 2 - 1) as g:
                gu_load(1, g * 2, g - 1)
                dn_load(g * 2, g * 2 - 1)
                gu_load(0, g * 2 + 1, g - 1)
                dn_load(g * 2 + 1, g * 2)
            gu_load(1, NE - 2, NE // 2 - 2)
            dn_load(NE - 2, NE - 3)
            sp.wait_ge(gu_used[1], NE // 2 * KD)
            sp.dma_start(bdn, b_dn[0]).then_inc(tail_in, 16)
            sp.dma_start(gfin, g_final.partition_broadcast(P)).then_inc(gfin_in, 16)
            gu_load(0, NE - 1, NE // 2 - 2)
            dn_load(NE - 1, NE - 2)
            sp.wait_ge(q_ok, 1)
            n_x = sp.value_load(qi[0:1, XCOLS:XCOLS + 1], min_val=0, max_val=XCOLS - 1)
            with sp.If(n_x > 0):
                with sp.Fori(0, n_x) as q:
                    e = sp.value_load(qi[0:1, bass.ds(q, 1)], min_val=0, max_val=NE - 1)
                    gu_load(0, e, q + (NE // 2 - 1))
                    dn_load(e, q + (NE - 1))
            for t in range(TT):
                for b in range(2):
                    h = slice(512 * b, 512 * b + 512)
                    sp.wait_ge(out_ok, 2 * t + b + 1)
                    sp.dma_start(out[0, t * P:(t + 1) * P, h], outb[:, t, h]).then_inc(out_done, 16)
            sp.wait_ge(out_done, 32 * TT)

        @block.gpsimd
        def _(pool):
            for r, n, src in vec_rows[7:]:
                pool.dma_start(vrow[r:r + n, :], src).then_inc(vec_in_pool, 16)

            def bias_load(c):
                at = slice(BC * c, BC * c + BC)
                for part in range(3):
                    pool.dma_start(stage[part * NE:(part + 1) * NE, c % 2, :], b_gu[0, :, at]).then_inc(bias_in[c % 2], 16)

            bias_load(0)
            bias_load(1)
            pool.dma_start(wr[:, :, :], w_router[0].rearrange("(k p) e -> p k e", p=P)).then_inc(route_in, 16)
            pool.dma_start(brow, b_router[0].partition_broadcast(P)).then_inc(route_in, 16)
            pool.wait_ge(uT_ps, KD)
            nc.gpsimd.memset(bdiag[:, :, :], 0.0).then_inc(bd_zero, 1)
            pool.wait_ge(bd_zero, 1)
            for w, src in enumerate((lwa, lwx)):
                s4 = src[0].rearrange("(c h) i j -> h i c j", h=2)
                for h in range(2):
                    pool.dma_start(bdiag[64 * h:64 * h + 64, CC * w:CC * (w + 1), 64 * h:64 * h + 64], s4[h]).then_inc(lruw_in, 16)
            steps = 0
            for c in range(F2 // BC):
                at = slice(BC * c, BC * c + BC)
                st = stage[:, c % 2, :]
                pool.wait_ge(bias_in[c % 2], 48 * (c // 2 + 1))
                for part in range(3):
                    for r0 in range(part, 3) if part else (0,):
                        rows_ = slice(r0 * NE, (r0 + 1) * NE) if part else slice(0, CAND)
                        nc.gpsimd.tensor_copy(biasp[rows_, at], st[rows_, :]).then_inc(pool_step, 1)
                        steps += 1
                        pool.wait_ge(pool_step, steps)
                    if part < 2:
                        rows_ = slice(2 * NE, 3 * NE) if part else slice(0, CAND)
                        nc.gpsimd.tensor_tensor(st[rows_, :], st[rows_, :], biasp[rows_, at], ALU.subtract).then_inc(pool_step, 1)
                        steps += 1
                        pool.wait_ge(pool_step, steps)
                if c + 2 < F2 // BC:
                    bias_load(c + 2)

        bias_steps = F2 // BC * 6

        @block.scalar
        def _(act):
            act.dma_start(metah, meta).then_inc(meta_in, 16)
            act.dma_start(grow[0:KD, :], g_mix[0].rearrange("(k n) -> k n", k=KD)).then_inc(vec_in, 16)
            act.dma_start(grow[KD:2 * KD, :], g_ffn[0].rearrange("(k n) -> k n", k=KD)).then_inc(vec_in, 16)
            for r, n, src in vec_rows[4:7]:
                act.dma_start(vrow[r:r + n, :], src).then_inc(vec_in, 16)
            act.wait_ge(ms_ok, 1)
            nc.scalar.activation(rstd, rstd, ACT.Sqrt).then_inc(rt_ok, 1)
            act.wait_ge(rinv0_ok, 1)
            nc.scalar.activation(unat[:, 1, :], xh[:, 1, :], ACT.Copy, scale=rstd[:, 1:2]).then_inc(un_ok, 1)
            act.wait_ge(sp_dve, 1)
            nc.scalar.activation(spt[1], spt[0], ACT.Exp, scale=-1.0).then_inc(sp_act, 1)
            act.wait_ge(vec_ok, 1)
            for k in range(1, KD, 2):
                act.wait_ge(uT_ps, k + 1)
                nc.scalar.activation(uT[:, k, :], bank[k][:, 0:T], ACT.Copy, scale=gcol(k)).then_inc(uT_act, 1)
            def diagonals(lo, hi):
                for k in range(lo, hi):
                    nc.scalar.activation(diag[:, k, :], ident, ACT.Copy, scale=col(V_CW + k, CC - 1)).then_inc(diag_ok, 1)

            for c in range(CC):
                act.wait_ge(z_ps, c + 1)
                if c:
                    act.wait_ge(z_dve, c)
                nc.scalar.activation(sig, bank[2 * (c % 2) + 1][:, 0:T], ACT.Sigmoid).then_inc(z_act, 1)
                if c == 1:
                    diagonals(0, TAPS // 2)
                if c == 2:
                    diagonals(TAPS // 2, TAPS)

            def lru_copies(c):
                act.wait_ge(z_ps, CC + c + 1)
                b = 2 * (c % 2)
                nc.scalar.activation(rx[:, c, 3:3 + T], bank[b][:, 0:T], ACT.Copy).then_inc(z_act, 1)
                nc.scalar.activation(rg[:, c, META:], bank[b + 1][:, META:T], ACT.Copy).then_inc(z_act, 1)

            def lru_gate(c):
                act.wait_ge(lg_ps, c + 1)
                nc.scalar.activation(ltau[:, c, :], bank[6][:, 0:T], ACT.Sigmoid, bias=col(V_BA, c)).then_inc(lg_act, 1)
                nc.scalar.activation(li[:, c, :], bank[7][:, 0:T], ACT.Sigmoid, bias=col(V_BX, c)).then_inc(lg_act, 1)
                act.wait_ge(lg_act, 3 * c + 1)
                nc.scalar.activation(ltau[:, c, :], ltau[:, c, :], ACT.Tanh, scale=sp4[:, c:c + 1]).then_inc(lg_act, 1)

            def lru_sqrt(c):
                act.wait_ge(rinv_ok, c + 2)
                act.wait_ge(lg_act, 3 * (c + 2))
                nc.scalar.activation(ltau[:, c:c + 2, :], ltau[:, c:c + 2, :], ACT.Sqrt, scale=4.0).then_inc(sq_ok, 1)

            lru_copies(0)
            act.wait_ge(c3_ps, 1)
            nc.scalar.activation(yc[:, CC - 1, :], bank[4][:, 0:SEQ], ACT.Identity, bias=col(V_CB, CC - 1)).then_inc(c3_ok, 1)
            act.wait_ge(sp_dve, 2)
            lru_gate(0)
            act.wait_ge(xc_ok, 1)
            nc.scalar.activation(lnsq, yc[:, :, :], ACT.Square).then_inc(sq2_ok, 1)
            lru_copies(1)
            act.wait_ge(lnv_ok, 1)
            nc.scalar.activation(acc2, acc2, ACT.Sqrt).then_inc(lns_ok, 1)
            act.wait_ge(yn_ok, 1)
            for c in range(CC):
                nc.scalar.activation(lnsq[:, c, :], yc[:, c, :], ACT.Sigmoid, bias=col(V_LB, c), scale=col(V_LG, c)).then_inc(lsig_ok, 1)
            lru_copies(2)
            lru_gate(1)
            lru_sqrt(0)
            lru_copies(3)
            act.wait_ge(z_act, CC + 2 * CC)
            nc.scalar.activation(rg[:, :, META:], rg[:, :, META:], ACT.Gelu_apprx_tanh).then_inc(gelu_ok, 1)
            lru_gate(2)
            lru_gate(3)
            lru_sqrt(2)
            def h_square(t):
                act.wait_ge(h_ok, 2 * t + 2)
                nc.scalar.activation(xn[:, t, :], xh[:, t, :], ACT.Square, accum_out=ssq2[:, t:t + 1]).then_inc(ss2_ok, 1)

            def h_copy(t, b):
                act.wait_ge(hT_ps, 2 * t + b + 1)
                nc.scalar.activation(hT[:, t, 4 * b:4 * b + 4, :], bank[4 + 2 * t + b][:, :].rearrange("p (k n) -> p k n", k=4), ACT.Copy).then_inc(hT_ok, 1)

            def h_root(t):
                act.wait_ge(ms2_ok, t + 1)
                nc.scalar.activation(rstd2[:, t:t + 1], rstd2[:, t:t + 1], ACT.Sqrt).then_inc(rt2_ok, 1)

            def h_normal(t):
                act.wait_ge(rinv2_ok, t + 1)
                nc.scalar.activation(xn[:, t, :], xh[:, t, :], ACT.Copy, scale=rstd2[:, t:t + 1]).then_inc(xn_ok, 1)

            h_square(0)
            h_root(0)
            h_copy(0, 0)
            h_copy(0, 1)
            h_normal(0)
            h_copy(1, 0)
            h_copy(1, 1)
            h_square(1)
            h_root(1)
            h_normal(1)
            act.wait_ge(ex_in, 1)
            nc.scalar.activation(ex[:, :, :], ex[:, :, :], ACT.Exp).then_inc(ex_ok, 1)

            def expert(n, first=False):
                act.wait_ge(gT_ps, n + 1)
                if not first:
                    act.wait_ge(acc_ps, n)
                nc.scalar.activation(gT, tb[:, 0:SEQ], ACT.Copy).then_inc(gT_ok, 1)
                act.wait_ge(glu_ok, n + 1)
                nc.scalar.activation(sigm, xglu, ACT.Sigmoid, scale=1.702).then_inc(sg_ok, 1)
                act.wait_ge(aT_ps, n + 1)
                nc.scalar.activation(actT, tb[:, :], ACT.Copy).then_inc(aT_ok, 1)
                act.wait_ge(y_ps, n + 1)
                nc.scalar.activation(yv, db[:, :], ACT.Copy).then_inc(y_ok, 1)

            expert(0, first=True)
            with act.Fori(1, NE) as n:
                expert(n)
            act.wait_ge(q_ok, 1)
            n_x = act.value_load(qi[0:1, XCOLS:XCOLS + 1], min_val=0, max_val=XCOLS - 1)
            with act.If(n_x > 0):
                with act.Fori(0, n_x) as q:
                    expert(q + NE)
            nc.scalar.activation(tiny[:, 38:39], tiny[:, 39:40], ACT.Sqrt).then_inc(fin_ss, 1)
            act.wait_ge(bd_ps, 1)
            for t in range(TT):
                for b in range(2):
                    nc.scalar.activation(outb[:, t, 512 * b:512 * b + 512], accb[t][b][:, :], ACT.Square,
                                         accum_out=ssq3[:, 2 * t + b:2 * t + b + 1]).then_inc(fin_ss, 1)
            for t in range(TT):
                act.wait_ge(ms3_ok, t + 1)
                nc.scalar.activation(rstd3[:, t:t + 1], rstd3[:, t:t + 1], ACT.Sqrt).then_inc(rt3_ok, 1)

        @block.vector
        def _(v):
            step = [0]

            def link(ins):
                step[0] += 1
                ins.then_inc(dv, 1)
                v.wait_ge(dv, step[0])

            def mark(ins):
                step[0] += 1
                ins.then_inc(dv, 1)
                return step[0]

            V = nc.vector
            link(V.memset(ssq[:, 2:3], 1.0))
            link(V.memset(tiny[:, 39:40], 1.0))
            link(V.memset(gpad[:, :, 0:TAPS - 1], 0.0))
            v.wait_ge(meta_in, 16)
            link(V.tensor_tensor_reduce(out=reg2[0:META, 0:D], in0=metah, in1=metah, scale=1.0, scalar=0.0,
                                        op0=ALU.mult, op1=ALU.add, accum_out=ssq[0:META, 2:3]))
            v.wait_ge(x_in, 32)
            for t in range(TT):
                link(V.tensor_tensor_reduce(out=unat[:, t, :], in0=xh[:, t, :], in1=xh[:, t, :], scale=1.0, scalar=0.0,
                                            op0=ALU.mult, op1=ALU.add, accum_out=ssq[:, t:t + 1]))
            V.tensor_scalar(rstd, ssq, 1.0 / D, NEG_EPS, ALU.mult, ALU.add).then_inc(ms_ok, 1)
            v.wait_ge(rt_ok, 1)
            V.reciprocal(rstd, rstd).then_inc(rinv0_ok, 1)
            v.wait_ge(rinv0_ok, 1)
            V.tensor_scalar(metah, metah, rstd[0:META, 2:3], None, ALU.mult).then_inc(un_ok, 1)
            V.tensor_scalar(unat[:, 0, :], xh[:, 0, :], rstd[:, 0:1], None, ALU.mult).then_inc(un_ok, 1)
            v.wait_ge(vecT, 1)
            V.tensor_copy(colv[:, :], bank[7][:, 0:CC * NV + NG]).then_inc(vec_ok, 1)
            v.wait_ge(vec_ok, 1)
            lamc = colv[:, 0:CC * NV].rearrange("p (c n) -> p c n", c=CC)[:, :, V_LAM]
            link(V.tensor_scalar(spt[3], lamc, -1.0, 0.0, ALU.mult, ALU.max))
            link(V.tensor_scalar(spt[2], lamc, 0.0, None, ALU.max))
            V.tensor_tensor(spt[0], spt[3], spt[2], ALU.add).then_inc(sp_dve, 1)
            for k in range(0, KD, 2):
                v.wait_ge(uT_ps, k + 1)
                V.tensor_scalar(uT[:, k, :], bank[k][:, 0:T], gcol(k), None, ALU.mult).then_inc(uT_dve, 1)
            v.wait_ge(sp_act, 1)
            link(V.tensor_scalar(spt[2], spt[1], 2.0, None, ALU.add))
            link(V.reciprocal(spt[2], spt[2]))
            link(V.tensor_tensor(spt[1], spt[1], spt[2], ALU.mult))
            link(V.tensor_tensor(spt[2], spt[1], spt[1], ALU.mult))
            link(V.memset(spt[0], 1.0 / 17))
            for d in (15, 13, 11, 9, 7, 5, 3, 1):
                link(V.tensor_tensor(spt[0], spt[0], spt[2], ALU.mult))
                link(V.tensor_scalar(spt[0], spt[0], 1.0 / d, None, ALU.add))
            link(V.tensor_tensor(spt[0], spt[0], spt[1], ALU.mult))
            link(V.scalar_tensor_tensor(spt[0], spt[0], 2.0, spt[3], ALU.mult, ALU.add))
            V.tensor_scalar(sp4, spt[0], 4.0, None, ALU.mult).then_inc(sp_dve, 1)

            def glu(c):
                v.wait_ge(z_act, c + 1)
                V.tensor_tensor(gpad[:, c, TAPS - 1:TAPS - 1 + T], bank[2 * (c % 2)][:, 0:T], sig, ALU.mult).then_inc(z_dve, 1)

            glu(0)
            between = {(0, 17): 1, (1, 4): 2, (1, 22): 3}
            for c in range(CC - 1):
                v.wait_ge(z_dve, c + 1)
                two_sums = [yc[:, c, :], acc2]
                last = [0, 0]
                for k in range(TAPS):
                    src = gpad[:, c, META + k:META + k + SEQ]
                    a = two_sums[k % 2]
                    if k == 0:
                        last[0] = mark(V.tensor_scalar(a, src, col(V_CW, c), col(V_CB, c), ALU.mult, ALU.add))
                    elif k == 1:
                        last[1] = mark(V.tensor_scalar(a, src, col(V_CW + 1, c), None, ALU.mult))
                    else:
                        v.wait_ge(dv, last[k % 2])
                        last[k % 2] = mark(V.scalar_tensor_tensor(a, src, col(V_CW + k, c), a, ALU.mult, ALU.add))
                    if (c, k) in between:
                        glu(between[c, k])
                v.wait_ge(dv, step[0])
                V.tensor_tensor(yc[:, c, :], yc[:, c, :], acc2, ALU.add).then_inc(yc_ok, 1)
                v.wait_ge(yc_ok, c + 1)

            def lru_conv(c):
                v.wait_ge(z_act, CC + 2 * c + 2)
                link(V.tensor_scalar(lu[:, c, :], rx[:, c, 0:T], col(V_LW, c), col(V_LCB, c), ALU.mult, ALU.add))
                for k in range(1, LTAPS):
                    ins = V.scalar_tensor_tensor(lu[:, c, :], rx[:, c, k:k + T], col(V_LW + k, c), lu[:, c, :], ALU.mult, ALU.add)
                    if k < LTAPS - 1:
                        link(ins)
                    else:
                        ins.then_inc(lu_ok, 1)

            def lru_in(c):
                v.wait_ge(lg_act, 3 * c + 3)
                link(V.tensor_scalar(lr[:, c, :], ltau[:, c, :], 1.0, None, ALU.add))
                V.reciprocal(lr[:, c, :], lr[:, c, :]).then_inc(rinv_ok, 1)
                v.wait_ge(lu_ok, c + 1)
                link(V.tensor_tensor(li[:, c, :], li[:, c, :], lu[:, c, :], ALU.mult))

            def lru_scan(c0):
                cs = slice(c0, c0 + 2)
                v.wait_ge(sq_ok, c0 // 2 + 1)
                v.wait_ge(rinv_ok, c0 + 2)
                link(V.tensor_tensor(ltau[:, cs, :], ltau[:, cs, :], lr[:, cs, :], ALU.mult))
                link(V.memset(ltau[:, cs, 0:1], 1.0))
                link(V.tensor_tensor(li[:, cs, :], li[:, cs, :], ltau[:, cs, :], ALU.mult))
                link(V.tensor_scalar(lr[:, cs, :], lr[:, cs, :], 2.0, -1.0, ALU.mult, ALU.add))
                for c in range(c0, c0 + 2):
                    link(V.tensor_tensor_scan(lu[:, c, :], lr[:, c, :], li[:, c, :], 0.0, ALU.mult, ALU.add))

            v.wait_ge(z_ps, CC)
            link(V.memset(rx[:, :, 0:3], 0.0))
            lru_conv(0)
            v.wait_ge(mean_ps, 1)
            mean = bank[4][:, 0:SEQ].unsqueeze(1).to_broadcast([P, CC, SEQ])
            V.scalar_tensor_tensor(yc[:, :, :], mean, -1.0 / CW, yc[:, :, :], ALU.mult, ALU.add).then_inc(xc_ok, 1)
            lru_conv(1)
            v.wait_ge(var_ps, 1)
            V.tensor_scalar(acc2, bank[5][:, 0:SEQ], 1.0 / CW, LN_EPS, ALU.mult, ALU.add).then_inc(lnv_ok, 1)
            v.wait_ge(lns_ok, 1)
            link(V.reciprocal(acc2, acc2))
            V.tensor_tensor(yc[:, :, :], yc[:, :, :], acc2.unsqueeze(1).to_broadcast([P, CC, SEQ]), ALU.mult).then_inc(yn_ok, 1)
            lru_in(0)
            v.wait_ge(lsig_ok, CC)
            for c in range(CC):
                link(V.tensor_scalar(yc[:, c, :], yc[:, c, :], col(V_LG, c), col(V_LB, c), ALU.mult, ALU.add))
            V.tensor_tensor(mixT[:, 0:CC, :], yc[:, :, :], lnsq, ALU.mult).then_inc(mix_ok, 1)
            lru_conv(2)
            lru_in(1)
            lru_scan(0)
            lru_conv(3)
            v.wait_ge(gelu_ok, 1)
            V.tensor_tensor(rg[:, 0:2, META:], lu[:, 0:2, META:], rg[:, 0:2, META:], ALU.mult).then_inc(mix_ok, 1)
            lru_in(2)
            lru_in(3)
            lru_scan(2)
            V.tensor_tensor(mixT[:, CC + 2:, :], lu[:, 2:, META:], rg[:, 2:, META:], ALU.mult).then_inc(mix_ok, 1)
            def one_hot(n):
                for t in range(TT):
                    ins = V.tensor_scalar(onehot[:, t, :], slot_no[:, 0:SLOTS], post[:, t, bass.ds(n, 1)], None, ALU.is_equal)
                ins.then_inc(oh_ok, 1)

            v.wait_ge(route_in, 32)
            for k in range(KD):
                ins = V.tensor_scalar(wr[:, k, :], wr[:, k, :], gcol(KD + k), None, ALU.mult)
            ins.then_inc(wr_ok, 1)
            def h_sum(t, b):
                v.wait_ge(h_ps, 2 * t + b + 1)
                V.tensor_tensor(xh[:, t, 512 * b:512 * b + 512], bank[2 * t + b][:, :], xh[:, t, 512 * b:512 * b + 512], ALU.add).then_inc(h_ok, 1)

            def h_rstd(t):
                ts = slice(t, t + 1)
                v.wait_ge(ss2_ok, t + 1)
                V.tensor_scalar(rstd2[:, ts], ssq2[:, ts], 1.0 / D, NEG_EPS, ALU.mult, ALU.add).then_inc(ms2_ok, 1)
                v.wait_ge(rt2_ok, t + 1)
                V.reciprocal(rstd2[:, ts], rstd2[:, ts]).then_inc(rinv2_ok, 1)
                v.wait_ge(rinv2_ok, t + 1)

            def lg_copy(t):
                v.wait_ge(lgT_ps, t + 1)
                V.tensor_copy(lgT[:, t * P:(t + 1) * P], bank[0][0:NE, t * P:(t + 1) * P]).then_inc(lgT_ok, 1)

            def top4(t):
                v.wait_ge(lg2_ps, t + 1)
                link(V.scalar_tensor_tensor(lg[:, t, :], bank[1][:, NE * t:NE * (t + 1)], rstd2[:, t:t + 1], brow, ALU.mult, ALU.add))
                link(V.max(mx[:, t, :], lg[:, t, :]))
                v4 = mx[:, t, TOPK - 1:TOPK]
                link(V.tensor_scalar(gt[:, t, :], lg[:, t, :], v4, None, ALU.is_gt))
                link(V.tensor_scalar(eq[:, t, :], lg[:, t, :], v4, None, ALU.is_equal))
                link(V.tensor_reduce(cnt[:, t, :], gt[:, t, :], axis=AX.X, op=ALU.add))
                link(V.tensor_tensor_scan(ceq[:, t, :], ones[:, 0:NE], eq[:, t, :], cnt[:, t, :], ALU.mult, ALU.add))
                link(V.scalar_tensor_tensor(eq[:, t, :], ceq[:, t, :], float(TOPK), eq[:, t, :], ALU.is_le, ALU.mult))
                V.tensor_tensor(mask[:, t, :], gt[:, t, :], eq[:, t, :], ALU.add).then_inc(mask_ok, 1)

            h_sum(0, 0)
            h_sum(0, 1)
            h_rstd(0)
            h_sum(1, 0)
            h_sum(1, 1)
            lg_copy(0)
            top4(0)
            h_rstd(1)
            lg_copy(1)
            top4(1)
            v.wait_ge(mask_ok, 2)
            v.wait_ge(pos_ps, 1)
            pos_v = bank[3][:, 0:TT * NE].rearrange("p (t e) -> p t e", t=TT)
            link(V.scalar_tensor_tensor(post[:, :, 0:NE], pos_v, 1.0, mask[:, :, :], ALU.add, ALU.mult))
            one_hot(0)
            V.tensor_tensor(ex[:, :, :], lg[:, :, :], mx[:, :, 0:1].to_broadcast([P, TT, NE]), ALU.subtract).then_inc(ex_in, 1)
            for b in range(3):
                link(V.tensor_copy(selt[b * NE:(b + 1) * NE, 0:NE], ident[b * NE:(b + 1) * NE, b * NE:(b + 1) * NE]))
            v.wait_ge(ex_ok, 1)
            link(V.tensor_tensor(ex[:, :, :], ex[:, :, :], mask[:, :, :], ALU.mult))
            link(V.tensor_reduce(den[:, :, 0], ex[:, :, :], axis=AX.X, op=ALU.add))
            link(V.reciprocal(den[:, :, :], den[:, :, :]))
            link(V.tensor_tensor(gatet[:, :, 0:NE], ex[:, :, :], den[:, :, 0:1].to_broadcast([P, TT, NE]), ALU.mult))
            c9 = slice(0, CAND)

            def gathered(n):
                v.wait_ge(gath_ps, n + 1)
                V.tensor_tensor(xgT[:, :, :], db[:, :].rearrange("p (k s) -> p k s", k=KD),
                                colv[:, CC * NV + KD:].unsqueeze(2).to_broadcast([P, KD, SLOTS]), ALU.mult).then_inc(xg_ok, 1)
                V.tensor_scalar(selb[0:CAND, :], ones[0:CAND, 0:SLOTS], selt[0:CAND, bass.ds(n, 1)], None, ALU.mult).then_inc(xg_ok, 1)

            gathered(0)
            v.wait_ge(x_pe, 1)
            V.tensor_scalar(fx[c9, 0:1], bank[2][c9, 0:1], cst[c9, C_THRC:C_THRC + 1], None, ALU.is_gt).then_inc(x_dve, 1)

            def list_places():
                v.wait_ge(x_pe, 2)
                link(V.tensor_copy(fx[c9, 1:2], bank[2][c9, 1:2]))
                V.tensor_scalar(sel96, cst[c9, C_IOTA:C_IOTA + XCOLS], fx[c9, 1:2], fx[c9, 0:1], ALU.is_equal, ALU.mult).then_inc(x_dve, 1)

            base = step[0] + 1

            def expert(n, s, use, between=None):
                one_hot(n + 1)
                for t in range(TT):
                    ins = V.tensor_scalar(wonehot[:, t, :], slot_no, post[:, t, bass.ds(n, 1)], gatet[:, t, bass.ds(n, 1)], ALU.is_equal, ALU.mult)
                ins.then_inc(oh_ok, 1)
                if between:
                    between()
                v.wait_ge(gu_used[s], use * KD)
                for b in range(2):
                    glu_v = gub[b][:, :].rearrange("p (n two) -> p n two", two=2)
                    h = slice(256 * b, 256 * b + 256)
                    ins = V.tensor_scalar(xglu[:, h], glu_v[:, :, 0], 7.0, None, ALU.min)
                ins.then_inc(glu_ok, 1)
                for b in range(2):
                    glu_v = gub[b][:, :].rearrange("p (n two) -> p n two", two=2)
                    h = slice(256 * b, 256 * b + 256)
                    ins = V.tensor_scalar(lin[:, h], glu_v[:, :, 1], 7.0, -7.0, ALU.min, ALU.max)
                ins.then_inc(gu_read, 1)
                v.wait_ge(gu_read, n + 1)
                v.wait_ge(glu_ok, n + 1)
                V.scalar_tensor_tensor(lin, lin, 1.0, xglu, ALU.add, ALU.mult).then_inc(dv, 1)
                v.wait_ge(dv, n + (base + 1))
                v.wait_ge(sg_ok, n + 1)
                V.tensor_tensor(actv, lin, sigm, ALU.mult).then_inc(act_ok, 1)
                gathered(n + 1)

            expert(0, 1, 1, between=list_places)
            v.wait_ge(x_pe, 3)
            V.tensor_copy(postT, tb[0:NE, 0:SEQ])
            V.tensor_copy(gateT, tb[0:NE, SEQ:2 * SEQ])
            V.tensor_copy(sel32, db[0:NE, 0:XCOLS])
            V.tensor_copy(selt[c9, NE:], db[c9, XCOLS:2 * XCOLS])
            V.tensor_copy(qi[0:1, :], db[0:1, 2 * XCOLS:3 * XCOLS + 1]).then_inc(x_dve, 1)
            expert(1, 0, 1)
            v.wait_ge(x_pe, 4)
            for i, table in enumerate((post, gatet)):
                src = db[:, 2 * XCOLS * i:2 * XCOLS * (i + 1)].rearrange("p (t q) -> p t q", t=TT)
                ins = V.tensor_copy(table[:, :, NE:], src)
            ins.then_inc(q_ok, 1)
            v.wait_ge(q_ok, 1)
            with v.Fori(1, NE // 2) as g:
                expert(g * 2, 1, g + 1)
                expert(g * 2 + 1, 0, g + 1)
            v.wait_ge(q_ok, 1)
            n_x = v.value_load(qi[0:1, XCOLS:XCOLS + 1], min_val=0, max_val=XCOLS - 1)
            with v.If(n_x > 0):
                with v.Fori(0, n_x) as q:
                    expert(q + NE, 0, q + (NE // 2 + 1))
            v.wait_ge(gfin_in, 16)
            for t in range(TT):
                ts = slice(t, t + 1)
                v.wait_ge(fin_ss, 2 * t + 3)
                V.tensor_tensor(rstd3[:, ts], ssq3[:, 2 * t:2 * t + 1], ssq3[:, 2 * t + 1:2 * t + 2], ALU.add).then_inc(fin_dve, 1)
                v.wait_ge(fin_dve, 2 * t + 1)
                V.tensor_scalar(rstd3[:, ts], rstd3[:, ts], 1.0 / D, NEG_EPS, ALU.mult, ALU.add).then_inc(ms3_ok, 1)
                v.wait_ge(rt3_ok, t + 1)
                V.reciprocal(rstd3[:, ts], rstd3[:, ts]).then_inc(fin_dve, 1)
                v.wait_ge(fin_dve, 2 * t + 2)
                for b in range(2):
                    h = slice(512 * b, 512 * b + 512)
                    V.scalar_tensor_tensor(outb[:, t, h], accb[t][b][:, :], rstd3[:, ts], gfin[:, h], ALU.mult, ALU.mult).then_inc(out_ok, 1)

        @block.tensor
        def _(pe):
            mm = nc.tensor.matmul
            pe.wait_ge(cst_in, 16)
            pe.wait_ge(vec_in, 16 * 9)
            pe.wait_ge(vec_in_pool, 16 * 2)
            for c in range(CC):
                nc.tensor.transpose(bank[7][:, c * NV:(c + 1) * NV], vrow[:, c * P:(c + 1) * P], ident[0:NV, 0:NV])
            nc.tensor.transpose(bank[7][:, CC * NV:CC * NV + NG], grow, ident[0:NG, 0:NG]).then_inc(vecT, 1)
            pe.wait_ge(un_ok, 3)
            for k in range(KD):
                ks = slice(k * P, (k + 1) * P)
                if k == KD - 1:
                    pe.wait_ge(vec_ok, 1)
                nc.tensor.transpose(bank[k][:, 0:META], metah[:, ks], ident[0:META, 0:META])
                for t in range(TT):
                    ins = nc.tensor.transpose(bank[k][:, META + t * P:META + (t + 1) * P], unat[:, t, ks], ident)
                ins.then_inc(uT_ps, 1)
            pe.wait_ge(uT_dve, KD // 2)
            pe.wait_ge(uT_act, KD // 2)

            def z_piece(p):
                pe.wait_ge(win_in[p], 32)
                if 2 <= p < 6:
                    pe.wait_ge(z_dve, p - 1)
                if p >= 6:
                    pe.wait_ge(z_act, CC + 2 * (p - 5))
                w = gu_ring[:, 0, p, :].rearrange("p (k b n) -> p k b n", k=KD, b=2)
                for b in range(2):
                    t0 = META if b and p >= CC else 0
                    for k in range(KD):
                        ins = mm(bank[2 * (p % 2) + b][:, t0:T], w[:, k, b, :], uT[:, k, t0:], start=(k == 0), stop=(k == KD - 1))
                ins.then_inc(z_ps, 1)

            def lru_gates(c):
                pe.wait_ge(lu_ok, c + 1)
                if c:
                    pe.wait_ge(lg_act, 3 * c - 1)
                mm(bank[6][:, 0:T], bdiag[:, c, :], lu[:, c, :], start=True, stop=True)
                mm(bank[7][:, 0:T], bdiag[:, CC + c, :], lu[:, c, :], start=True, stop=True).then_inc(lg_ps, 1)

            for p in range(CC + 1):
                z_piece(p)
            pe.wait_ge(z_dve, CC)
            for k in range(TAPS):
                if k == 0:
                    pe.wait_ge(diag_ok, TAPS // 2)
                if k == TAPS // 2:
                    pe.wait_ge(diag_ok, TAPS)
                ins = mm(bank[4][:, 0:SEQ], diag[:, k, :], gpad[:, CC - 1, META + k:META + k + SEQ],
                         start=(k == 0), stop=(k == TAPS - 1))
            ins.then_inc(c3_ps, 1)
            pe.wait_ge(lruw_in, 64)
            lru_gates(0)
            pe.wait_ge(yc_ok, CC - 1)
            pe.wait_ge(c3_ok, 1)
            for c in range(CC):
                ins = mm(bank[4][:, 0:SEQ], ones, yc[:, c, :], start=(c == 0), stop=(c == CC - 1))
            ins.then_inc(mean_ps, 1)
            z_piece(CC + 1)
            pe.wait_ge(sq2_ok, 1)
            for c in range(CC):
                ins = mm(bank[5][:, 0:SEQ], ones, lnsq[:, c, :], start=(c == 0), stop=(c == CC - 1))
            ins.then_inc(var_ps, 1)
            z_piece(CC + 2)
            lru_gates(1)
            z_piece(CC + 3)
            lru_gates(2)

            def out_proj(t, b, k):
                if k in (CC, CC + 1):
                    m = rg[:, k - CC, META + t * P:META + (t + 1) * P]
                else:
                    m = mixT[:, k, t * P:(t + 1) * P]
                return mm(bank[2 * t + b][:, :], m, dn_ring[:, k, 512 * b:512 * b + 512],
                          start=(k == 0), stop=(k == KD - 1))

            pe.wait_ge(z_act, CC + 2 * CC)
            pe.wait_ge(mix_ok, 1)
            for k in range(CC + 2):
                if k == CC:
                    pe.wait_ge(mix_ok, 2)
                if k % 2 == 0:
                    pe.wait_ge(wout_in[k // 2], 16)
                for t in range(TT):
                    for b in range(2):
                        ins = out_proj(t, b, k)
                if k % 2:
                    ins.then_inc(wout_used, 1)
                if k == 1:
                    lru_gates(3)
            pe.wait_ge(mix_ok, 3)
            pe.wait_ge(wout_in[3], 16)

            def h_turned(t, b):
                pe.wait_ge(h_ok, 2 * t + b + 1)
                for k in range(4):
                    kk = 4 * b + k
                    ins = nc.tensor.transpose(bank[4 + 2 * t + b][:, k * P:(k + 1) * P], xh[:, t, kk * P:(kk + 1) * P], ident)
                ins.then_inc(hT_ps, 1)

            def logits(t):
                pe.wait_ge(hT_ok, 2 * t + 2)
                for k in range(KD):
                    ins = mm(bank[0][0:NE, t * P:(t + 1) * P], wr[:, k, :], hT[:, t, k, :], start=(k == 0), stop=(k == KD - 1))
                ins.then_inc(lgT_ps, 1)

            def logits_back(t):
                pe.wait_ge(lgT_ok, t + 1)
                nc.tensor.transpose(bank[1][:, NE * t:NE * (t + 1)], lgT[:, t * P:(t + 1) * P], ident[0:NE, 0:NE]).then_inc(lg2_ps, 1)

            for b in range(2):
                for k in range(CC + 2, KD):
                    ins = out_proj(0, b, k)
                ins.then_inc(h_ps, 1)
            for k in range(CC + 2, KD):
                ins = out_proj(1, 0, k)
            ins.then_inc(h_ps, 1)
            h_turned(0, 0)
            h_turned(0, 1)
            for k in range(CC + 2, KD):
                ins = out_proj(1, 1, k)
            ins.then_inc(h_ps, 1)
            pe.wait_ge(wr_ok, 1)
            h_turned(1, 0)
            logits(0)
            h_turned(1, 1)
            logits_back(0)
            logits(1)
            logits_back(1)
            pe.wait_ge(mask_ok, 1)
            mm(bank[3][:, 0:NE], tri, mask[:, 0, :], start=True, stop=True)
            mm(bank[3][:, NE:2 * NE], ones, mask[:, 0, :], start=True, stop=False)
            pe.wait_ge(mask_ok, 2)
            mm(bank[3][:, NE:2 * NE], tri, mask[:, 1, :], start=False, stop=True).then_inc(pos_ps, 1)

            def gather(n, after):
                pe.wait_ge(oh_ok, after)
                for k in range(KD):
                    for t in range(TT):
                        ins = mm(db[:, k * SLOTS:(k + 1) * SLOTS], xn[:, t, k * P:(k + 1) * P], onehot[:, t, :],
                                 start=(t == 0), stop=(t == TT - 1))
                ins.then_inc(gath_ps, 1)

            pe.wait_ge(xn_ok, TT)
            gather(0, 1)
            for b in range(EXTRA):
                for t in range(TT):
                    ins = mm(bank[2][b * NE:(b + 1) * NE, 0:1], mask[:, t, :], ones[:, 0:1], start=(t == 0), stop=(t == TT - 1))
            ins.then_inc(x_pe, 1)
            c9 = slice(0, CAND)
            pe.wait_ge(pool_step, bias_steps)

            def expert(n, s, loads, first=False, between=None, before_turn=None, before_down=None):
                pe.wait_ge(xg_ok, n * 2 + 2)
                if not first:
                    pe.wait_ge(gu_read, n)
                for b in range(2):
                    for h in range(2):
                        mm(gub[b][64 * h:64 * h + 64, :], selb[0:CAND, :], biasp[:, 1024 * h + 512 * b:1024 * h + 512 * b + 512],
                           start=True, stop=False)
                for j in range(KD):
                    pe.wait_ge(gu_in[s][j], loads * 16)
                    for b in range(2):
                        for h in range(2):
                            ins = mm(gub[b][64 * h:64 * h + 64, :], xgT[:, j, :],
                                     gu_ring[:, s, j, 1024 * h + 512 * b:1024 * h + 512 * b + 512],
                                     start=False, stop=(j == KD - 1))
                    ins.then_inc(gu_used[s], 1)
                    if j == KD // 2 and between:
                        between()
                if before_turn:
                    before_turn()
                pe.wait_ge(oh_ok, n * 2 + 3)
                for t in range(TT):
                    ins = nc.tensor.transpose(tb[:, t * P:(t + 1) * P], wonehot[:, t, :], ident)
                ins.then_inc(gT_ps, 1)
                gather(n + 1, n * 2 + 3)
                pe.wait_ge(act_ok, n + 1)
                pe.wait_ge(gT_ok, n + 1)
                for c in range(4):
                    ins = nc.tensor.transpose(tb[:, c * P:(c + 1) * P], actv[:, c * P:(c + 1) * P], ident)
                ins.then_inc(aT_ps, 1)
                if before_down:
                    before_down()
                pe.wait_ge(aT_ok, n + 1)
                pe.wait_ge(xg_ok, n * 2 + 4)
                for k in range(KD):
                    if k % 2 == 0:
                        pe.wait_ge(dn_in[k // 2], n * 16 + 16)
                    at = (k % 4) * P + (k // 4) * SLOTS
                    for h in range(2):
                        ins = mm(db[64 * h:64 * h + 64, :], actT[:, at:at + SLOTS], dn_ring[:, k, 512 * h:512 * h + 512],
                                 start=(k == 0), stop=(k == KD - 1))
                    if k % 2 and k < KD - 1:
                        ins.then_inc(dn_used, 1)
                ins.then_inc(y_ps, 1)
                pe.wait_ge(y_ok, n + 1)
                for t in range(TT):
                    for h in range(2):
                        ins = mm(accb[t][h][:, :], gT[64 * h:64 * h + 64, t * P:(t + 1) * P], yv[64 * h:64 * h + 64, :],
                                 start=first, stop=True, skip_group_check=True)
                ins.then_inc(acc_ps, 1)

            def list_places():
                pe.wait_ge(x_dve, 1)
                mm(bank[2][c9, 1:2], cst[c9, C_TRI96:C_TRI96 + CAND], fx[c9, 0:1], start=True, stop=True).then_inc(x_pe, 1)

            def wait_places():
                pe.wait_ge(x_dve, 2)

            def wait_list():
                pe.wait_ge(x_dve, 3)

            def add_b_down():
                pe.wait_ge(tail_in, 16)
                for t in range(TT):
                    for b in range(2):
                        mm(accb[t][b][:, :], gateT[:, t * P:(t + 1) * P], bdn[:, 512 * b:512 * b + 512],
                           start=False, stop=True, skip_group_check=True)
                        mm(accb[t][b][:, :], ident, xh[:, t, 512 * b:512 * b + 512],
                           start=False, stop=True, skip_group_check=True)

            expert(0, 1, 1, first=True, between=list_places, before_down=wait_places)
            for i, table in enumerate((post, gatet)):
                for t in range(TT):
                    nc.tensor.transpose(tb[0:NE, i * SEQ + t * P:i * SEQ + (t + 1) * P], table[:, t, 0:NE], ident)
            mm(db[0:NE, 0:XCOLS], cst[c9, C_RR:C_RR + NE], sel96, start=True, stop=True)
            mm(db[c9, XCOLS:2 * XCOLS], cst[c9, C_RR:C_RR + CAND], sel96, start=True, stop=True)
            mm(db[0:1, 2 * XCOLS:3 * XCOLS], cst[c9, C_EID:C_EID + 1], sel96, start=True, stop=True)
            mm(db[0:1, 3 * XCOLS:3 * XCOLS + 1], fx[c9, 0:1], ones[c9, 0:1], start=True, stop=True).then_inc(x_pe, 1)
            expert(1, 0, 1, before_turn=wait_list)
            for i, table in enumerate((postT, gateT)):
                for t in range(TT):
                    o_ = db[:, (2 * i + t) * XCOLS:(2 * i + t + 1) * XCOLS]
                    ins = mm(o_, table[:, t * P:(t + 1) * P], sel32, start=True, stop=(i == 1))
                    if i == 0:
                        ins = mm(o_, cst[c9, C_THRB:C_THRB + P], sel96, start=False, stop=True)
            ins.then_inc(x_pe, 1)
            pe.wait_ge(q_ok, 1)
            with pe.Fori(1, NE // 2 - 1) as g:
                expert(g * 2, 1, g + 1)
                expert(g * 2 + 1, 0, g + 1)
            expert(NE - 2, 1, NE // 2)
            add_b_down()
            expert(NE - 1, 0, NE // 2)
            n_x = pe.value_load(qi[0:1, XCOLS:XCOLS + 1], min_val=0, max_val=XCOLS - 1)
            with pe.If(n_x > 0):
                with pe.Fori(0, n_x) as q:
                    expert(q + NE, 0, q + (NE // 2 + 1))
            nc.tensor.matmul(db[:, 0:1], ones, ones[:, 0:1], start=True, stop=True).then_inc(bd_ps, 1)


def kernel(**inputs):
    import numpy as _np
    import concourse.bacc as _bacc
    from concourse import mybir as _mybir
    from concourse.bass_utils import run_bass_kernel_spmd as _run

    nc = _bacc.Bacc("TRN2", target_bir_lowering=False, num_devices=1)
    names = ["x", "meta_tokens", "g_mix", "w_in", "conv_dw_w", "conv_dw_b", "conv_ln_g", "conv_ln_b",
             "lru_conv_w", "lru_conv_b", "lru_wa", "lru_ba", "lru_wx", "lru_bx", "lru_lambda", "w_out",
             "g_ffn", "w_router", "b_router", "w_gate_up", "b_gate_up", "w_down", "b_down", "g_final"]
    arrays, args = {}, []
    for name in names + ["shape_constants"]:
        a = constants() if name == "shape_constants" else _np.ascontiguousarray(inputs[name])
        arrays[f"in_{name}"] = a
        args.append(nc.dram_tensor(f"in_{name}", a.shape, _mybir.dt.from_np(a.dtype), kind="ExternalInput").ap())
    out = nc.dram_tensor("out_0", (1, SEQ, D), _mybir.dt.float32, kind="ExternalOutput").ap()
    build(nc, *args, out)
    r = _run(nc, [arrays], core_ids=[0])
    return r.results[0]["out_0"]
```
